# Optimizing a Trainium2 kernel written in Bass

```python
import math
import jax
import jax.numpy as jnp
from jax import lax
import numpy as np

D_MODEL = 1024
BATCH = 1
SEQ = 2048
DEPTH = 1
DEC_BATCH = 8
DEC_SEQ = 1
PAST_LEN = 4096
PAGE_SIZE = 128

HEAD_DIM = 64
Q_BLOCK = 128
EPS = 1e-6
NEG_INF = -1e30
SCALE = HEAD_DIM ** -0.5
F32 = jnp.float32

A_WINDOWS = (128, 512, 2048)
A_DILATIONS = (1, 4, 16)
A_HPG = 2
A_HEADS = A_HPG * len(A_WINDOWS)
A_WIDTH = A_HEADS * HEAD_DIM
B_HEADS = 4
B_WIDTH = B_HEADS * HEAD_DIM
FGATE_BIAS0 = 8.0
C_HEADS = 6
C_INNER = C_HEADS * HEAD_DIM
C_GROUPS = 2
C_STATE = 128
C_CONV = 4
C_CONV_DIM = C_INNER + 2 * C_GROUPS * C_STATE
C_CHUNK = 128
MIX_WIDTH = A_WIDTH + B_WIDTH + C_INNER
D_FF = 2816
FFN_CONV = 3
REL_BUCKETS = 32
REL_MAX_DIST = 2048
IN_SIZES = (A_WIDTH, A_WIDTH, A_WIDTH, B_WIDTH, B_WIDTH, B_WIDTH, B_HEADS, C_INNER, C_CONV_DIM, C_HEADS)
IN_COLS = sum(IN_SIZES)
IN_SPLITS = tuple(int(s) for s in np.cumsum(IN_SIZES)[:-1])

kernel_name = "hybrid_dilated_fox_ssd_decoder_step"

def rmsnorm(x, w):
    xf = x.astype(F32)
    y = xf * lax.rsqrt(jnp.mean(xf * xf, axis=-1, keepdims=True) + EPS)
    return (y * w.astype(F32)).astype(x.dtype)

def causal_dwconv(xpad, w, bias):
    K = w.shape[0]
    T = xpad.shape[1] - K + 1
    y = bias
    for j in range(K):
        y = y + xpad[:, j:j + T] * w[j]
    return y

def t5_bucket(dist):
    exact = REL_BUCKETS // 2
    far = exact + (jnp.log(jnp.maximum(dist, 1).astype(F32) / exact)
                   / math.log(REL_MAX_DIST / exact) * (REL_BUCKETS - exact)).astype(jnp.int32)
    return jnp.where(dist < exact, dist, jnp.minimum(far, REL_BUCKETS - 1))

def in_project(h, w_in, fgate_b):
    b, T = h.shape[:2]
    aq, ak, av, bq, bk, bv, fl, cz, cxbc, cdt = jnp.split(h @ w_in, IN_SPLITS, axis=-1)
    hd = lambda t: t.reshape(b, T, -1, HEAD_DIM)
    logf = jax.nn.log_sigmoid(fl.astype(F32) + fgate_b.astype(F32))
    return hd(aq), hd(ak), hd(av), hd(bq), hd(bk), hd(bv), logf, cz, cxbc, cdt

def dilated_attend(q, kb, vb, bias, valid):
    s = jnp.einsum('bthe,btnhe->bthn', q, kb, preferred_element_type=F32) * SCALE + bias.T.astype(F32)
    s = jnp.where(valid[:, None, :], s, NEG_INF)
    m = jnp.max(s, axis=-1, keepdims=True)
    p = jnp.exp(s - m)
    den = jnp.sum(p, axis=-1)
    o = jnp.einsum('bthn,btnhe->bthe', p, vb.astype(F32)) / den[..., None]
    return o, m[..., 0] + jnp.log(den)

def merge_dilations(outs, lses):
    alpha = jax.nn.softmax(jnp.stack(lses, axis=0), axis=0)
    return jnp.concatenate([o * a[..., None] for o, a in zip(outs, alpha)], axis=2)

def dilated_prompt(q, k, v, rel_bias):
    b, L = q.shape[:2]
    outs, lses, bufs = [], [], []
    for g, (W, d) in enumerate(zip(A_WINDOWS, A_DILATIONS)):
        hs = slice(g * A_HPG, (g + 1) * A_HPG)
        qg, kg, vg = q[:, :, hs], k[:, :, hs], v[:, :, hs]
        offs = jnp.arange(W // d + 1, dtype=jnp.int32) * d
        bias = rel_bias[t5_bucket(offs)][:, hs]
        pad = ((0, 0), (W, 0), (0, 0), (0, 0))
        kp, vp = jnp.pad(kg, pad), jnp.pad(vg, pad)
        local = W + jnp.arange(Q_BLOCK)[:, None] - offs[None, :]

        def block(i):
            t0 = i * Q_BLOCK
            qb = lax.dynamic_slice_in_dim(qg, t0, Q_BLOCK, axis=1)
            kw = lax.dynamic_slice_in_dim(kp, t0, W + Q_BLOCK, axis=1)
            vw = lax.dynamic_slice_in_dim(vp, t0, W + Q_BLOCK, axis=1)
            valid = (t0 + jnp.arange(Q_BLOCK))[:, None] - offs[None, :] >= 0
            return dilated_attend(qb, jnp.take(kw, local, axis=1), jnp.take(vw, local, axis=1), bias, valid)

        o, lse = lax.map(block, jnp.arange(L // Q_BLOCK))
        outs.append(o.transpose(1, 0, 2, 3, 4).reshape(b, L, A_HPG, HEAD_DIM))
        lses.append(lse.transpose(1, 0, 2, 3).reshape(b, L, A_HPG))
        bufs.append(jnp.stack([kg, vg], axis=2)[:, L - min(W, L):])
    return merge_dilations(outs, lses).reshape(b, L, A_WIDTH).astype(q.dtype), bufs

def dilated_decode(q, k, v, bufs, rel_bias):
    b, T = q.shape[:2]
    outs, lses, new_bufs = [], [], []
    for g, (W, d) in enumerate(zip(A_WINDOWS, A_DILATIONS)):
        hs = slice(g * A_HPG, (g + 1) * A_HPG)
        buf = bufs[g]
        Lg = buf.shape[1]
        kv = jnp.concatenate([buf.astype(k.dtype), jnp.stack([k[:, :, hs], v[:, :, hs]], axis=2)], axis=1)
        offs = jnp.arange(W // d + 1, dtype=jnp.int32) * d
        bias = rel_bias[t5_bucket(offs)][:, hs]
        idx = Lg + jnp.arange(T)[:, None] - offs[None, :]
        g_kv = jnp.take(kv, jnp.maximum(idx, 0), axis=1)
        o, lse = dilated_attend(q[:, :, hs], g_kv[:, :, :, 0], g_kv[:, :, :, 1], bias, idx >= 0)
        outs.append(o)
        lses.append(lse)
        new_bufs.append(kv[:, T:])
    return merge_dilations(outs, lses).reshape(b, T, A_WIDTH).astype(q.dtype), new_bufs

def fox_prompt(q, k, v, logf):
    b, L, H, e = q.shape
    cum = jnp.cumsum(logf, axis=1).transpose(0, 2, 1)
    vf = v.astype(F32)
    kpos = jnp.arange(L)

    def block(i):
        t0 = i * Q_BLOCK
        qb = lax.dynamic_slice_in_dim(q, t0, Q_BLOCK, axis=1)
        cq = lax.dynamic_slice_in_dim(cum, t0, Q_BLOCK, axis=2)
        s = jnp.einsum('bqhe,bkhe->bhqk', qb, k, preferred_element_type=F32) * SCALE
        s = s + cq[..., :, None] - cum[:, :, None, :]
        s = jnp.where((t0 + jnp.arange(Q_BLOCK))[:, None] >= kpos[None, :], s, NEG_INF)
        return jnp.einsum('bhqk,bkhe->bqhe', jax.nn.softmax(s, axis=-1), vf)

    o = lax.map(block, jnp.arange(L // Q_BLOCK))
    return o.transpose(1, 0, 2, 3, 4).reshape(b, L, H * e).astype(q.dtype)

def fox_decode(q, k, v, logf, kv_pool, logf_pool, page_table):
    b, T, H, e = q.shape
    past = kv_pool[page_table]
    S = past.shape[1] * past.shape[2]
    past = past.reshape(b, S, 2, H, e)
    lf_past = logf_pool[page_table].reshape(b, S, H).astype(F32)
    suffix = lax.cumsum(lf_past, axis=1, reverse=True) - lf_past
    cn = jnp.cumsum(logf, axis=1).transpose(0, 2, 1)
    s_past = jnp.einsum('bthe,bshe->bhts', q, past[:, :, 0].astype(q.dtype), preferred_element_type=F32) * SCALE
    s_past = s_past + suffix.transpose(0, 2, 1)[:, :, None, :] + cn[..., :, None]
    s_new = jnp.einsum('bthe,bshe->bhts', q, k, preferred_element_type=F32) * SCALE
    s_new = s_new + cn[..., :, None] - cn[..., None, :]
    s_new = jnp.where(jnp.tril(jnp.ones((T, T), bool)), s_new, NEG_INF)
    p = jax.nn.softmax(jnp.concatenate([s_past, s_new], axis=-1), axis=-1)
    o = (jnp.einsum('bhts,bshe->bthe', p[..., :S], past[:, :, 1].astype(F32))
         + jnp.einsum('bhts,bshe->bthe', p[..., S:], v.astype(F32)))
    return o.reshape(b, T, H * e).astype(q.dtype)

def segsum(a):
    T = a.shape[-1]
    xr = jnp.broadcast_to(a[..., :, None], a.shape + (T,))
    xr = jnp.where(jnp.tril(jnp.ones((T, T), bool), -1), xr, 0.0)
    ss = jnp.cumsum(xr, axis=-2)
    return jnp.where(jnp.tril(jnp.ones((T, T), bool)), ss, -jnp.inf)

def ssd_scan(x, dt, A, Bm, Cm, h0):
    b, T, H, P = x.shape
    N = Bm.shape[-1]
    Q = min(C_CHUNK, T)
    pad = (-T) % Q
    if pad:
        padT = lambda z: jnp.pad(z, [(0, 0), (0, pad)] + [(0, 0)] * (z.ndim - 2))
        x, dt, Bm, Cm = padT(x), padT(dt), padT(Bm), padT(Cm)
    nc = (T + pad) // Q
    xd = (x * dt[..., None]).reshape(b, nc, Q, H, P)
    Bc = Bm.reshape(b, nc, Q, H, N)
    Cc = Cm.reshape(b, nc, Q, H, N)
    a = (dt * A).reshape(b, nc, Q, H).transpose(0, 3, 1, 2)
    a_cs = jnp.cumsum(a, axis=-1)
    scores = jnp.einsum('bclhn,bcshn->bhcls', Cc, Bc) * jnp.exp(segsum(a))
    y_diag = jnp.einsum('bhcls,bcshp->bclhp', scores, xd)
    decay_states = jnp.exp(a_cs[..., -1:] - a_cs)
    states = jnp.einsum('bclhn,bhcl,bclhp->bchpn', Bc, decay_states, xd)
    chunk_decay = jnp.exp(a_cs[..., -1])

    def step(h, inp):
        s_c, d_c = inp
        return h * d_c[..., None, None] + s_c, h

    final, prev = lax.scan(step, h0, (states.transpose(1, 0, 2, 3, 4), chunk_decay.transpose(2, 0, 1)))
    prev = prev.transpose(1, 0, 2, 3, 4)
    y_off = jnp.einsum('bclhn,bchpn,bhcl->bclhp', Cc, prev, jnp.exp(a_cs))
    y = (y_diag + y_off).reshape(b, nc * Q, H, P)[:, :T]
    return y, final

def ssd_mixer(z, xbc, dt_raw, conv_buf, h0, conv_w, conv_b, dt_bias, A_log, D_skip, norm_w):
    b, T = z.shape[:2]
    xpad = jnp.concatenate([conv_buf.astype(xbc.dtype), xbc], axis=1)
    xbc_c = jax.nn.silu(causal_dwconv(xpad, conv_w, conv_b))
    new_buf = xpad[:, -(C_CONV - 1):]
    xs, Bm, Cm = jnp.split(xbc_c, [C_INNER, C_INNER + C_GROUPS * C_STATE], axis=-1)
    hpg = C_HEADS // C_GROUPS
    xs = xs.reshape(b, T, C_HEADS, HEAD_DIM).astype(F32)
    Bm = jnp.repeat(Bm.reshape(b, T, C_GROUPS, C_STATE), hpg, axis=2).astype(F32)
    Cm = jnp.repeat(Cm.reshape(b, T, C_GROUPS, C_STATE), hpg, axis=2).astype(F32)
    dt = jax.nn.softplus(dt_raw.astype(F32) + dt_bias.astype(F32))
    A = -jnp.exp(A_log.astype(F32))
    y, h_new = ssd_scan(xs, dt, A, Bm, Cm, h0.astype(F32))
    y = y + D_skip.astype(F32)[:, None] * xs
    y = y.reshape(b, T, C_INNER) * jax.nn.silu(z.astype(F32))
    return rmsnorm(y, norm_w).astype(z.dtype), h_new, new_buf

def conv_ffn(h, buf, w_up, conv_w, conv_b, w_down):
    gate, up = jnp.split(h @ w_up, 2, axis=-1)
    gpad = jnp.concatenate([buf.astype(gate.dtype), gate], axis=1)
    g = causal_dwconv(gpad, conv_w, conv_b)
    return (jax.nn.silu(g) * up) @ w_down, gpad[:, -(FFN_CONV - 1):]

def layer(x, rel_bias, ln_mix_w, w_in, fgate_b, conv_w, conv_b, dt_bias, A_log, D_skip,
          ssm_norm_w, w_out, ln_ffn_w, w_up, ffn_conv_w, ffn_conv_b, w_down, past=None):
    b = x.shape[0]
    aq, ak, av, bq, bk, bv, logf, cz, cxbc, cdt = in_project(rmsnorm(x, ln_mix_w), w_in, fgate_b)
    if past is None:
        a_out, win_new = dilated_prompt(aq, ak, av, rel_bias)
        b_out = fox_prompt(bq, bk, bv, logf)
        h0 = jnp.zeros((b, C_HEADS, HEAD_DIM, C_STATE), F32)
        conv_buf = jnp.zeros((b, C_CONV - 1, C_CONV_DIM), x.dtype)
        ffn_buf = jnp.zeros((b, FFN_CONV - 1, D_FF), x.dtype)
    else:
        win_bufs, fox_kv, fox_logf, page_table, h0, conv_buf, ffn_buf = past
        a_out, win_new = dilated_decode(aq, ak, av, win_bufs, rel_bias)
        b_out = fox_decode(bq, bk, bv, logf, fox_kv, fox_logf, page_table)
    c_out, h_new, conv_new = ssd_mixer(cz, cxbc, cdt, conv_buf, h0, conv_w, conv_b,
                                       dt_bias, A_log, D_skip, ssm_norm_w)
    x = x + jnp.concatenate([a_out, b_out, c_out], axis=-1) @ w_out
    f, ffn_new = conv_ffn(rmsnorm(x, ln_ffn_w), ffn_buf, w_up, ffn_conv_w, ffn_conv_b, w_down)
    x = x + f
    return x, (win_new[0], win_new[1], win_new[2], jnp.stack([bk, bv], axis=2), logf, h_new, conv_new, ffn_new)

def setup_inputs(seed: int = 0) -> dict:
    key = jax.random.key(seed)
    ks = iter(jax.random.split(key, 40))
    nrm = lambda shape, scale=1.0: scale * jax.random.normal(next(ks), shape, F32)
    n_pages = PAST_LEN // PAGE_SIZE
    n_pool = (DEC_BATCH * n_pages * 5) // 4
    perm = jax.random.permutation(next(ks), n_pool).astype(jnp.int32)
    page_table = perm[:DEC_BATCH * n_pages].reshape(DEC_BATCH, n_pages)
    dt0 = jnp.exp(jax.random.uniform(next(ks), (DEPTH, C_HEADS), F32, math.log(1e-3), math.log(1e-1)))
    a0 = jax.random.uniform(next(ks), (DEPTH, C_HEADS), F32, 1.0, 16.0)
    return {
        "x_prompt": nrm((BATCH, SEQ, D_MODEL)),
        "x_sample": nrm((DEC_BATCH, DEC_SEQ, D_MODEL)),
        "cache_win0": nrm((DEPTH, DEC_BATCH, min(A_WINDOWS[0], PAST_LEN), 2, A_HPG, HEAD_DIM)),
        "cache_win1": nrm((DEPTH, DEC_BATCH, min(A_WINDOWS[1], PAST_LEN), 2, A_HPG, HEAD_DIM)),
        "cache_win2": nrm((DEPTH, DEC_BATCH, min(A_WINDOWS[2], PAST_LEN), 2, A_HPG, HEAD_DIM)),
        "cache_fox_kv": nrm((DEPTH, n_pool, PAGE_SIZE, 2, B_HEADS, HEAD_DIM)),
        "cache_fox_logf": jax.nn.log_sigmoid(FGATE_BIAS0 + nrm((DEPTH, n_pool, PAGE_SIZE, B_HEADS), 0.5)),
        "state_ssm": nrm((DEPTH, DEC_BATCH, C_HEADS, HEAD_DIM, C_STATE), 0.5),
        "state_ssm_conv": nrm((DEPTH, DEC_BATCH, C_CONV - 1, C_CONV_DIM)),
        "state_ffn_conv": nrm((DEPTH, DEC_BATCH, FFN_CONV - 1, D_FF)),
        "page_table": page_table,
        "rel_bias": nrm((REL_BUCKETS, A_HEADS), 0.5),
        "ln_mix_w": 1.0 + nrm((DEPTH, D_MODEL), 0.02),
        "w_in": nrm((DEPTH, D_MODEL, IN_COLS), D_MODEL ** -0.5),
        "fox_fgate_b": FGATE_BIAS0 + nrm((DEPTH, B_HEADS), 0.5),
        "ssm_conv_w": nrm((DEPTH, C_CONV, C_CONV_DIM), C_CONV ** -0.5),
        "ssm_conv_b": nrm((DEPTH, C_CONV_DIM), 0.02),
        "ssm_dt_bias": dt0 + jnp.log(-jnp.expm1(-dt0)),
        "ssm_A_log": jnp.log(a0),
        "ssm_D": 1.0 + nrm((DEPTH, C_HEADS), 0.1),
        "ssm_norm_w": 1.0 + nrm((DEPTH, C_INNER), 0.02),
        "w_out": nrm((DEPTH, MIX_WIDTH, D_MODEL), MIX_WIDTH ** -0.5),
        "ln_ffn_w": 1.0 + nrm((DEPTH, D_MODEL), 0.02),
        "w_up": nrm((DEPTH, D_MODEL, 2 * D_FF), D_MODEL ** -0.5),
        "ffn_conv_w": nrm((DEPTH, FFN_CONV, D_FF), FFN_CONV ** -0.5),
        "ffn_conv_b": nrm((DEPTH, D_FF), 0.02),
        "w_down": nrm((DEPTH, D_FF, D_MODEL), D_FF ** -0.5),
        "final_norm_w": 1.0 + nrm((D_MODEL,), 0.02),
    }

def reference(x_prompt, x_sample, cache_win0, cache_win1, cache_win2, cache_fox_kv, cache_fox_logf,
              state_ssm, state_ssm_conv, state_ffn_conv, page_table, rel_bias, ln_mix_w, w_in,
              fox_fgate_b, ssm_conv_w, ssm_conv_b, ssm_dt_bias, ssm_A_log, ssm_D, ssm_norm_w,
              w_out, ln_ffn_w, w_up, ffn_conv_w, ffn_conv_b, w_down, final_norm_w):
    y_prompt, y_sample = x_prompt, x_sample
    st_p, st_s = [], []
    for l in range(DEPTH):
        w = (ln_mix_w[l], w_in[l], fox_fgate_b[l], ssm_conv_w[l], ssm_conv_b[l], ssm_dt_bias[l],
             ssm_A_log[l], ssm_D[l], ssm_norm_w[l], w_out[l], ln_ffn_w[l], w_up[l],
             ffn_conv_w[l], ffn_conv_b[l], w_down[l])
        y_prompt, sp = layer(y_prompt, rel_bias, *w)
        past = ((cache_win0[l], cache_win1[l], cache_win2[l]), cache_fox_kv[l], cache_fox_logf[l],
                page_table, state_ssm[l], state_ssm_conv[l], state_ffn_conv[l])
        y_sample, ss = layer(y_sample, rel_bias, *w, past=past)
        st_p.append(sp)
        st_s.append(ss)
    y_prompt = rmsnorm(y_prompt, final_norm_w)
    y_sample = rmsnorm(y_sample, final_norm_w)
    p_win0, p_win1, p_win2, p_fox_kv, p_fox_logf, p_ssm, p_ssm_conv, p_ffn_conv = [
        jnp.stack([s[i] for s in st_p], axis=0) for i in range(8)]
    s_win0, s_win1, s_win2, s_fox_kv, s_fox_logf, s_ssm, s_ssm_conv, s_ffn_conv = [
        jnp.stack([s[i] for s in st_s], axis=0) for i in range(8)]
    return (y_prompt, y_sample, p_win0, p_win1, p_win2, p_fox_kv, p_fox_logf, p_ssm, p_ssm_conv, p_ffn_conv,
            s_win0, s_win1, s_win2, s_fox_kv, s_fox_logf, s_ssm, s_ssm_conv, s_ffn_conv)


_drawn_inputs = setup_inputs


def setup_inputs(seed=0):
    import zlib

    import numpy as np

    out = dict(_drawn_inputs(seed))
    spreads = {}
    factors = {'cache_fox_kv': 4.25,
     'cache_fox_logf': 200.0,
     'rel_bias': 3.223,
     'ssm_norm_w': 5.083,
     'ln_ffn_w': 2.803,
     'ffn_conv_b': 6.207,
     'final_norm_w': 27.96}
    for name, (base, spread) in spreads.items():
        noise = np.random.default_rng([zlib.crc32(name.encode()), seed]).standard_normal(out[name].shape)
        drawn = base * np.exp(spread * noise) if base else spread * noise
        out[name] = jnp.asarray(drawn.astype(out[name].dtype))
    for name, factor in factors.items():
        out[name] = (out[name] * factor).astype(out[name].dtype)
    return out
```

```python
from contextlib import ExitStack, contextmanager

import numpy as np
import concourse.bass as bass
from concourse import mybir

F32 = mybir.dt.float32
F32R = mybir.dt.float32r
BF16 = mybir.dt.bfloat16
I32 = mybir.dt.int32
ALU = mybir.AluOpType
ACT = mybir.ActivationFunctionType
AX = mybir.AxisListType

P = 128
D_MODEL = 1024
KT = D_MODEL // P
SEQ = 2048
DEC = 8
TILES = SEQ // P
ALL_TILES = TILES + 1
PAST = 4096
PAGE = 128
PAGES = PAST // PAGE
HD = 64
EPS = 1e-6
NEG = -1e30
SCALE = HD ** -0.5
WINDOWS = (128, 512, 2048)
DILATIONS = (1, 4, 16)
GROUPS = len(WINDOWS)
A_WIDTH = 384
B_HEADS = 4
B_WIDTH = B_HEADS * HD
C_HEADS = 6
C_INNER = C_HEADS * HD
C_GROUPS = 2
C_STATE = 128
C_CONV = 4
CONV_DIM = C_INNER + 2 * C_GROUPS * C_STATE
D_FF = 2816
FF_TILES = D_FF // P
FFN_CONV = 3
BUCKETS = 32
AQ, AK, AV = 0, A_WIDTH, 2 * A_WIDTH
BQ = 3 * A_WIDTH
BK, BV, FL = BQ + B_WIDTH, BQ + 2 * B_WIDTH, BQ + 3 * B_WIDTH
COLS_A = FL + B_HEADS
CZ, CX, CDT = 0, C_INNER, C_INNER + CONV_DIM
COLS_B = CDT + C_HEADS
MIX_A = A_WIDTH + 4 * GROUPS


class Steps:

    def __init__(self, sem):
        self.sem, self.base, self.n = sem, 0, 0

    def mark(self, ins, by=1):
        ins.then_inc(self.sem, by)
        self.n += by

    def link(self, eng, ins):
        self.mark(ins)
        eng.wait_ge(self.sem, self.base + self.n)

    @contextmanager
    def loop(self, i, trips, per_trip):
        base = self.base + self.n
        self.base, self.n = i * per_trip + base, 0
        yield
        assert self.n == per_trip, (self.n, per_trip)
        self.base, self.n = base + trips * per_trip, 0


def over_tiles(eng, body, steps=None, per_pair=0):
    body(0, 0, 1)
    with eng.Fori(0, TILES // 2) as i:
        if steps:
            with steps.loop(i, TILES // 2, per_pair):
                body(i * 2 + 1, 1, i + 1)
                body(i * 2 + 2, 0, i + 2)
        else:
            body(i * 2 + 1, 1, i + 1)
            body(i * 2 + 2, 0, i + 2)


def rows(ap, t, n=P):
    return ap[bass.ds(t * P, n), :]


def project(nc, tag, w_d, xT_d, x_d, lnw_d, out_d, widths, rstd_all, first):
    cols = sum(widths)
    nb = len(widths)
    starts = [sum(widths[:k]) for k in range(nb)]
    with ExitStack() as ctx:
        def sb(name, shape, dt=F32):
            return ctx.enter_context(nc.sbuf_tensor(f"{tag}_{name}", shape, dt))

        def sem(name):
            return ctx.enter_context(nc.semaphore(f"{tag}_{name}"))

        w_hi = sb("w_hi", [P, KT, cols], F32R)
        w_lo = sb("w_lo", [P, KT, cols], F32R)
        w_raw = sb("w_raw", [P, 2, cols])
        lnw = sb("lnw", [P, KT])
        xT = sb("xT", [P, 2, KT, P])
        hs = sb("hs", [P, KT, P])
        h_hi = sb("h_hi", [P, 2, KT, P], F32R)
        h_lo = sb("h_lo", [P, 2, KT, P], F32R)
        row = sb("row", [P, 2, cols])
        acc = ctx.enter_context(nc.psum_tensor(f"{tag}_acc", [P, 2, nb, 512], F32))
        rstd = sb("rstd", [P, 2])
        if first:
            x_tok = sb("x_tok", [P, 2, D_MODEL])
            junk = sb("junk", [P, D_MODEL])
            ssq = sb("ssq", [P, 2])
            root = sb("root", [P, 2])
            nt = sb("nt", [P, 4])

        w_landed = [sem(f"w_landed{k}") for k in range(2)]
        w_split = sem("w_split")
        lnw_landed = sem("lnw_landed")
        xT_landed = [sem(f"xT_landed{k}") for k in range(2)]
        h_split = sem("h_split")
        mm_done = sem("mm_done")
        evac = sem("evac")
        stored = [sem(f"stored{k}") for k in range(2)]
        dve = Steps(sem("dve"))
        if first:
            x_landed = [sem(f"x_landed{k}") for k in range(2)]
            squared = sem("squared")
            mean_ready = sem("mean_ready")
            rooted = sem("rooted")
        rstd_ready = sem("rstd_ready")
        block = ctx.enter_context(nc.Block())

        @block.sync
        def _(sp):
            sp.dma_start(lnw[:], lnw_d).then_inc(lnw_landed, 16)

            def load(t, slot, use):
                if not (isinstance(t, int) and t == 0):
                    sp.wait_ge(h_split, t)
                    if first:
                        sp.wait_ge(rstd_ready, t)
                sp.dma_start(xT[:, slot], xT_d[bass.ds(t, 1)].rearrange("a p k n -> (a p) k n")
                             ).then_inc(xT_landed[slot], 16)
                if first:
                    sp.dma_start(x_tok[:, slot], rows(x_d, t)).then_inc(x_landed[slot], 16)

            for k in range(KT):
                if k >= 2:
                    sp.wait_ge(w_split, k - 1)
                sp.dma_start(w_raw[:, k % 2], w_d[:, k]).then_inc(w_landed[k % 2], 16)
                if k == 1:
                    load(0, 0, 1)
            with sp.Fori(0, TILES // 2) as i:
                load(i * 2 + 1, 1, i + 1)
                load(i * 2 + 2, 0, i + 2)

        @block.scalar
        def _(act):
            for k in range(KT):
                act.wait_ge(w_landed[k % 2], 16 * (k // 2 + 1))
                act.activation(w_hi[:, k], w_raw[:, k % 2], ACT.Copy).then_inc(evac, 1)

            def body(t, slot, use):
                if first:
                    act.wait_ge(x_landed[slot], use * 16)
                    act.activation(junk[:], x_tok[:, slot], ACT.Square, accum_out=ssq[:, slot:slot + 1]
                                   ).then_inc(squared, 1)
                    act.wait_ge(mean_ready, t + 1)
                    act.activation(root[:, slot:slot + 1], ssq[:, slot:slot + 1], ACT.Sqrt).then_inc(rooted, 1)
                act.wait_ge(rstd_ready, t + 1)
                if not (isinstance(t, int) and t == 0):
                    act.wait_ge(stored[slot], use * 16 - (16 if slot == 0 else 0))
                for b in range(nb):
                    act.wait_ge(mm_done, t * nb + b + 1)
                    act.activation(row[:, slot, starts[b]:starts[b] + widths[b]], acc[:, slot, b, 0:widths[b]],
                                   ACT.Copy, scale=rstd[:, slot:slot + 1]).then_inc(evac, 1)
                act.wait_ge(evac, t * nb + nb + KT)
                act.dma_start(rows(out_d, t), row[:, slot]).then_inc(stored[slot], 16)

            act.sem_inc(stored[1], 16)
            over_tiles(act, body)
            act.wait_ge(stored[0], 16 * (TILES // 2 + 1))
            act.wait_ge(stored[1], 16 * (TILES // 2 + 1))

        @block.vector
        def _(v):
            for k in range(KT):
                v.wait_ge(w_landed[k % 2], 16 * (k // 2 + 1))
                v.wait_ge(evac, k + 1)
                v.tensor_tensor(w_lo[:, k], w_raw[:, k % 2], w_hi[:, k].bitcast(F32), ALU.subtract
                                ).then_inc(w_split, 1)

            def body(t, slot, use):
                v.wait_ge(xT_landed[slot], use * 16)
                if not (isinstance(t, int) and t == 0):
                    v.wait_ge(mm_done, (t - 1) * nb + 1)
                dve.link(v, v.tensor_tensor(hs[:], xT[:, slot], lnw[:].unsqueeze(2).to_broadcast([P, KT, P]),
                                            ALU.mult))
                dve.link(v, v.tensor_copy(h_hi[:, slot], hs[:]))
                v.tensor_tensor(h_lo[:, slot], hs[:], h_hi[:, slot].bitcast(F32), ALU.subtract
                                ).then_inc(h_split, 1)
                if first:
                    v.wait_ge(squared, t + 1)
                    dve.link(v, v.tensor_scalar(ssq[:, slot:slot + 1], ssq[:, slot:slot + 1], 1.0 / D_MODEL, EPS,
                                                ALU.mult, ALU.add))
                    v.tensor_copy(nt[:, 3:4], ssq[:, slot:slot + 1]).then_inc(mean_ready, 1)
                    v.wait_ge(rooted, t + 1)
                    dve.link(v, v.reciprocal(nt[:, 0:1], root[:, slot:slot + 1]))
                    dve.link(v, v.tensor_tensor(nt[:, 1:2], nt[:, 0:1], nt[:, 0:1], ALU.mult))
                    v.wait_ge(mean_ready, t + 1)
                    dve.link(v, v.tensor_tensor(nt[:, 2:3], nt[:, 1:2], nt[:, 3:4], ALU.mult))
                    dve.link(v, v.tensor_scalar(nt[:, 1:2], nt[:, 2:3], -0.5, 1.5, ALU.mult, ALU.add))
                    dve.link(v, v.tensor_tensor(rstd[:, slot:slot + 1], nt[:, 0:1], nt[:, 1:2], ALU.mult))
                    v.tensor_copy(rstd_all[:, bass.ds(t, 1)], rstd[:, slot:slot + 1]).then_inc(rstd_ready, 1)
                else:
                    if not (isinstance(t, int) and t == 0):
                        v.wait_ge(evac, t * nb - nb + KT)
                    v.tensor_copy(rstd[:, slot:slot + 1], rstd_all[:, bass.ds(t, 1)]).then_inc(rstd_ready, 1)
                v.wait_ge(h_split, t + 1)

            v.wait_ge(lnw_landed, 16)
            over_tiles(v, body, dve, 2 * (8 if first else 2))

        @block.tensor
        def _(pe):
            pe.wait_ge(w_split, KT)

            def body(t, slot, use):
                pe.wait_ge(h_split, t + 1)
                if not (isinstance(t, int) and t == 0):
                    pe.wait_ge(evac, t * nb - nb + KT)
                for b in range(nb):
                    cs = slice(starts[b], starts[b] + widths[b])
                    out = acc[:, slot, b, 0:widths[b]]
                    for k in range(KT):
                        pe.matmul(out, h_hi[:, slot, k], w_hi[:, k, cs], start=(k == 0), stop=False)
                        pe.matmul(out, h_hi[:, slot, k], w_lo[:, k, cs], start=False, stop=False)
                        last = pe.matmul(out, h_lo[:, slot, k], w_hi[:, k, cs], start=False, stop=(k == KT - 1))
                    last.then_inc(mm_done, 1)

            over_tiles(pe, body)


IDENT, TRI_LE, TRI_GT, CAUSAL, ONES, PAGE_AFTER = range(6)


def gate_values(nc, pa, pb, gate_bias_d, gates, logf_p_d, logf_s_d):
    G = B_HEADS + C_HEADS
    with ExitStack() as ctx:
        def sb(name, shape, dt=F32):
            return ctx.enter_context(nc.sbuf_tensor(f"gv_{name}", shape, dt))

        def sem(name):
            return ctx.enter_context(nc.semaphore(f"gv_{name}"))

        z = sb("z", [P, ALL_TILES, G])
        mag = sb("mag", [P, ALL_TILES, G])
        u = sb("u", [P, ALL_TILES, G])
        ratio = sb("ratio", [P, ALL_TILES, G])
        sq = sb("sq", [P, ALL_TILES, G])
        ser = sb("ser", [P, ALL_TILES, G])
        bias = sb("bias", [P, G])
        landed, mag_ready, exp_done, done, stored = (sem(n) for n in (
            "landed", "mag_ready", "exp_done", "done", "stored"))
        dve = Steps(sem("dve"))
        block = ctx.enter_context(nc.Block())

        @block.sync
        def _(sp):
            sp.dma_start(z[:, :, 0:B_HEADS], pa[:, FL:COLS_A].rearrange("(t p) c -> p t c", p=P)
                         ).then_inc(landed, 16)
            sp.dma_start(z[:, :, B_HEADS:G], pb[:, CDT:COLS_B].rearrange("(t p) c -> p t c", p=P)
                         ).then_inc(landed, 16)
            sp.dma_start(bias[:], gate_bias_d.rearrange("(a g) -> a g", a=1).broadcast_to([P, G])
                         ).then_inc(landed, 16)
            sp.wait_ge(done, 1)
            sp.dma_start(logf_p_d, gates[:, 1:ALL_TILES, 0:B_HEADS]).then_inc(stored, 16)
            sp.dma_start(logf_s_d, gates[0:DEC, 0, 0:B_HEADS]).then_inc(stored, 16)
            sp.wait_ge(stored, 32)

        @block.scalar
        def _(act):
            act.wait_ge(mag_ready, 1)
            act.activation(u[:], mag[:], ACT.Exp, scale=-1.0).then_inc(exp_done, 1)

        @block.vector
        def _(v):
            v.wait_ge(landed, 48)
            dve.link(v, v.tensor_tensor(z[:], z[:], bias[:].unsqueeze(1).to_broadcast([P, ALL_TILES, G]), ALU.add))
            dve.link(v, v.tensor_scalar(z[:, :, 0:B_HEADS], z[:, :, 0:B_HEADS], -1.0, None, ALU.mult))
            dve.link(v, v.tensor_scalar(mag[:], z[:], -1.0, None, ALU.mult))
            v.tensor_tensor(mag[:], mag[:], z[:], ALU.max).then_inc(mag_ready, 1)
            v.wait_ge(exp_done, 1)
            dve.link(v, v.tensor_scalar(ratio[:], u[:], 2.0, None, ALU.add))
            dve.link(v, v.reciprocal(ratio[:], ratio[:]))
            dve.link(v, v.tensor_tensor(ratio[:], ratio[:], u[:], ALU.mult))
            dve.link(v, v.tensor_tensor(sq[:], ratio[:], ratio[:], ALU.mult))
            dve.link(v, v.tensor_scalar(ser[:], sq[:], 1.0 / 17, None, ALU.mult))
            for k in (15, 13, 11, 9, 7, 5, 3):
                dve.link(v, v.scalar_tensor_tensor(out=ser[:], in0=ser[:], scalar=1.0 / k, in1=sq[:],
                                                   op0=ALU.add, op1=ALU.mult))
            dve.link(v, v.scalar_tensor_tensor(out=ser[:], in0=ser[:], scalar=1.0, in1=ratio[:],
                                               op0=ALU.add, op1=ALU.mult))
            dve.link(v, v.tensor_scalar(z[:], z[:], 0.0, None, ALU.max))
            dve.link(v, v.scalar_tensor_tensor(out=gates[:], in0=ser[:], scalar=2.0, in1=z[:],
                                               op0=ALU.mult, op1=ALU.add))
            v.tensor_scalar(gates[:, :, 0:B_HEADS], gates[:, :, 0:B_HEADS], -1.0, None, ALU.mult).then_inc(done, 1)


def fox_prompt(nc, pa, consts_d, gates, mb):
    AUG = HD + 2
    RING = 5
    banks = [(t + 4) // 4 for t in range(TILES)]
    before = [sum(banks[:t]) for t in range(TILES + 1)]
    NB = before[TILES]
    assert NB % RING == 0 and NB % 2 == 0
    with ExitStack() as ctx:
        def sb(name, shape, dt=F32):
            return ctx.enter_context(nc.sbuf_tensor(f"fp_{name}", shape, dt))

        def ps(name, shape):
            return ctx.enter_context(nc.psum_tensor(f"fp_{name}", shape, F32))

        def sem(name):
            return ctx.enter_context(nc.semaphore(f"fp_{name}"))

        consts = sb("consts", [P, 6, P])
        ident_b = sb("ident_b", [P, P], BF16)
        mask_b = sb("mask_b", [P, P], BF16)
        cum = sb("cum", [P, TILES, B_HEADS])
        lf = sb("lf", [P, TILES, B_HEADS])
        total = sb("total", [P, TILES, B_HEADS])
        raw = sb("raw", [P, 3, TILES, HD])
        q_tok = sb("q_tok", [P, TILES, AUG])
        k_tok = sb("k_tok", [P, TILES, AUG])
        v_tok = sb("v_tok", [P, TILES, HD])
        qT = sb("qT", [AUG, TILES * P])
        kT = sb("kT", [AUG, TILES * P])
        probs = sb("probs", [P, 2, TILES * P])
        pT = sb("pT", [P, 2, 512])
        o_tok = sb("o_tok", [P, TILES, HD])
        mx = sb("mx", [P, 2, 4])
        neg = sb("neg", [P, 2])
        den = sb("den", [P, 2, 4])
        rden = sb("rden", [P, 2])
        s_ps = ps("s", [P, RING, 512])
        t_ps = ps("t", [P, 2, 512])
        o_ps = ps("o", [P, 2, HD])

        consts_landed = sem("consts_landed")
        raw_landed = sem("raw_landed")
        raw_used = sem("raw_used")
        ready = sem("ready")
        cum_mm = sem("cum_mm")
        aug_ready = sem("aug_ready")
        tr_done = sem("tr_done")
        qk_ready = sem("qk_ready")
        qk = sem("qk")
        neg_ready = sem("neg_ready")
        exped = sem("exped")
        tp = sem("tp")
        pt_ready = [sem("pt_ready_even"), sem("pt_ready_odd")]
        pv = sem("pv")
        o_ready = sem("o_ready")
        stored = sem("stored")
        dve = Steps(sem("dve"))
        block = ctx.enter_context(nc.Block())

        @block.sync
        def _(sp):
            sp.dma_start(consts[:], consts_d).then_inc(consts_landed, 16)
            with sp.Fori(0, B_HEADS) as h:
                sp.wait_ge(raw_used, h + 1)
                for k, col in enumerate((BQ, BK, BV)):
                    sp.dma_start(raw[:, k], pa[P:, bass.ds(h * HD + col, HD)].rearrange(
                        "(t p) e -> p t e", p=P)).then_inc(raw_landed, 16)

        @block.vector
        def _(v):
            v.sem_inc(raw_used, 1)
            v.sem_inc(stored, 16)
            v.wait_ge(consts_landed, 16)
            v.tensor_copy(ident_b[:], consts[:, IDENT])
            v.tensor_copy(mask_b[:], consts[:, CAUSAL])
            v.tensor_copy(lf[:], gates[:, 1:ALL_TILES, 0:B_HEADS]).then_inc(ready, 1)
            v.wait_ge(cum_mm, 1)
            n = TILES * B_HEADS
            s_flat = s_ps[:, 0, 0:n].rearrange("p (t h) -> p t h", h=B_HEADS)
            t_flat = s_ps[:, 1, 0:n].rearrange("p (t h) -> p t h", h=B_HEADS)
            dve.link(v, v.memset(total[:, 0], 0.0))
            for t in range(1, TILES):
                dve.link(v, v.tensor_tensor(total[:, t], total[:, t - 1], t_flat[:, t - 1], ALU.add))
            dve.link(v, v.tensor_tensor(cum[:], s_flat, total[:], ALU.add))
            v.memset(q_tok[:, :, HD:HD + 1], 1.0)
            dve.link(v, v.memset(k_tok[:, :, HD + 1:AUG], 1.0))
            with v.Fori(0, B_HEADS) as h, dve.loop(h, B_HEADS, sum(1 + (b > 1) for b in banks) + 2 * TILES):
                v.wait_ge(raw_landed, h * 48 + 48)
                v.wait_ge(tr_done, h * 8 + 1)
                v.wait_ge(pv, h * NB + 2)
                v.tensor_copy(q_tok[:, :, HD + 1:AUG], cum[:, :, bass.ds(h, 1)])
                v.tensor_scalar(k_tok[:, :, HD:HD + 1], cum[:, :, bass.ds(h, 1)], -1.0, None, ALU.mult)
                v.tensor_copy(k_tok[:, :, 0:HD], raw[:, 1])
                v.tensor_copy(v_tok[:], raw[:, 2]).then_inc(aug_ready, 1)
                v.wait_ge(aug_ready, h * 2 + 2)
                v.sem_inc(raw_used, 1)
                for g in range(4):
                    v.wait_ge(tr_done, h * 8 + 2 * g + 2 + 1)
                    v.tensor_copy(kT[:, g * 512:(g + 1) * 512], t_ps[0:AUG, 1]).then_inc(qk_ready, 1)
                v.wait_ge(stored, h * 16 + 16)

                def maxima(t):
                    for b in range(banks[t]):
                        n = before[t] + b
                        w = min(512, (t + 1 - 4 * b) * P)
                        v.wait_ge(qk, h * NB + n + 1)
                        last = v.reduce_max(mx[:, t % 2, b:b + 1], s_ps[:, n % RING, 0:w], AX.X)
                    dve.link(v, last)
                    if banks[t] > 1:
                        dve.link(v, v.reduce_max(mx[:, t % 2, 0:1], mx[:, t % 2, 0:banks[t]], AX.X))
                    if t >= 2:
                        v.wait_ge(exped, h * NB + RING + before[t - 1])
                    v.tensor_scalar(neg[:, t % 2:t % 2 + 1], mx[:, t % 2, 0:1], -1.0, None, ALU.mult
                                    ).then_inc(neg_ready, 1)

                def evacuate(t):
                    for b in range(banks[t]):
                        n = before[t] + b
                        if n % 2 == 0:
                            w = min(512, (t + 1 - 4 * b) * P)
                            v.wait_ge(tp, h * NB + n + 1)
                            v.wait_ge(pv, h * NB + n + 1)
                            v.tensor_copy(pT[:, 0, 0:w], t_ps[:, 0, 0:w]).then_inc(pt_ready[0], 1)

                def finish(t):
                    v.wait_ge(exped, h * NB + RING + before[t + 1])
                    dve.link(v, v.reduce_sum(rden[:, t % 2:t % 2 + 1], den[:, t % 2, 0:banks[t]], AX.X))
                    dve.link(v, v.reciprocal(rden[:, t % 2:t % 2 + 1], rden[:, t % 2:t % 2 + 1]))
                    v.wait_ge(pv, h * NB + 2 + before[t + 1])
                    v.tensor_scalar(o_tok[:, t], o_ps[:, t % 2], rden[:, t % 2:t % 2 + 1], None, ALU.mult
                                    ).then_inc(o_ready, 1)

                for t in range(TILES + 1):
                    if t < TILES:
                        maxima(t)
                    if t >= 1:
                        evacuate(t - 1)
                        finish(t - 1)

        @block.scalar
        def _(act):
            act.sem_inc(exped, RING)
            with act.Fori(0, B_HEADS) as h:
                act.wait_ge(raw_landed, h * 48 + 48)
                act.wait_ge(tr_done, h * 8 + 1)
                act.activation(q_tok[:, :, 0:HD], raw[:, 0], ACT.Copy, scale=SCALE).then_inc(aug_ready, 1)
                for g in range(4):
                    act.wait_ge(tr_done, h * 8 + 2 * g + 1 + 1)
                    act.activation(qT[:, g * 512:(g + 1) * 512], t_ps[0:AUG, 0], ACT.Copy).then_inc(qk_ready, 1)

                def exps(t):
                    act.wait_ge(neg_ready, h * TILES + t + 1)
                    if t >= 2:
                        act.wait_ge(tp, h * NB + before[t - 1])
                        act.wait_ge(o_ready, h * TILES + t - 1)
                    for b in range(banks[t]):
                        n = before[t] + b
                        w = min(512, (t + 1 - 4 * b) * P)
                        act.activation(probs[:, t % 2, b * 512:b * 512 + w], s_ps[:, n % RING, 0:w], ACT.Exp,
                                       bias=neg[:, t % 2:t % 2 + 1],
                                       accum_out=den[:, t % 2, b:b + 1]).then_inc(exped, 1)

                def evacuate(t):
                    for b in range(banks[t]):
                        n = before[t] + b
                        if n % 2 == 1:
                            w = min(512, (t + 1 - 4 * b) * P)
                            act.wait_ge(tp, h * NB + n + 1)
                            act.wait_ge(pv, h * NB + n + 1)
                            act.activation(pT[:, 1, 0:w], t_ps[:, 1, 0:w], ACT.Copy).then_inc(pt_ready[1], 1)

                for t in range(TILES + 1):
                    if t < TILES:
                        exps(t)
                    if t >= 1:
                        evacuate(t - 1)
                act.wait_ge(o_ready, h * TILES + TILES)
                act.dma_start(mb[P:, bass.ds(h * HD, HD)].rearrange("(t p) e -> p t e", p=P), o_tok[:]
                              ).then_inc(stored, 16)
            act.wait_ge(stored, 16 * (B_HEADS + 1))

        @block.tensor
        def _(pe):
            pe.wait_ge(ready, 1)
            n = TILES * B_HEADS
            pe.matmul(s_ps[:, 0, 0:n], consts[:, TRI_LE], lf[:].rearrange("p t h -> p (t h)"), start=True, stop=True)
            pe.matmul(s_ps[:, 1, 0:n], consts[:, ONES], lf[:].rearrange("p t h -> p (t h)"), start=True, stop=True
                      ).then_inc(cum_mm, 1)
            pe.sem_inc(tr_done, 1)
            pe.sem_inc(pv, 2)
            with pe.Fori(0, B_HEADS) as h:
                pe.wait_ge(aug_ready, h * 2 + 2)
                for g in range(4):
                    for k, src in ((0, q_tok), (1, k_tok)):
                        if g >= 1:
                            pe.wait_ge(qk_ready, h * 8 + 2 * g)
                        for j in range(4):
                            last = pe.transpose(t_ps[0:AUG, k, j * P:(j + 1) * P], src[:, 4 * g + j],
                                                consts[:, IDENT])
                        last.then_inc(tr_done, 1)
                pe.wait_ge(qk_ready, h * 8 + 8)

                def scores(t):
                    for b in range(banks[t]):
                        n = before[t] + b
                        w = min(512, (t + 1 - 4 * b) * P)
                        pe.wait_ge(exped, h * NB + n + 1)
                        diag = b == banks[t] - 1
                        last = pe.matmul(s_ps[:, n % RING, 0:w], qT[:, t * P:(t + 1) * P],
                                         kT[:, b * 512:b * 512 + w], start=True, stop=not diag)
                        if diag:
                            last = pe.matmul(s_ps[:, n % RING, w - P:w], ident_b[:], mask_b[:], start=False, stop=True)
                        last.then_inc(qk, 1)

                def turn(t, b):
                    n = before[t] + b
                    pe.wait_ge(exped, h * NB + RING + n + 1)
                    if n >= 2:
                        pe.wait_ge(pt_ready[n % 2], h * (NB // 2) + n // 2)
                    for j in range(min(4, t + 1 - 4 * b)):
                        c = b * 512 + j * P
                        last = pe.transpose(t_ps[:, n % 2, j * P:(j + 1) * P], probs[:, t % 2, c:c + P],
                                            consts[:, IDENT])
                    last.then_inc(tp, 1)

                def values(t, b):
                    n = before[t] + b
                    pe.wait_ge(pt_ready[n % 2], h * (NB // 2) + n // 2 + 1)
                    if b == 0 and t >= 2:
                        pe.wait_ge(o_ready, h * TILES + t - 1)
                    for j in range(min(4, t + 1 - 4 * b)):
                        k = 4 * b + j
                        last = pe.matmul(o_ps[:, t % 2], pT[:, n % 2, j * P:(j + 1) * P], v_tok[:, k],
                                         start=(k == 0), stop=(k == t))
                    last.then_inc(pv, 1)

                for t in range(TILES + 1):
                    if t < TILES:
                        scores(t)
                    if t >= 1:
                        for b in range(banks[t - 1]):
                            turn(t - 1, b)
                            if b >= 1:
                                values(t - 1, b - 1)
                        values(t - 1, banks[t - 1] - 1)
                pe.wait_ge(o_ready, h * TILES + TILES)


BIAS_ROW = 384


def dilated_prompt(nc, pa, consts_d, rel_d, onehot_d, toep_d, ma, raw_landed):
    U = 4
    with ExitStack() as ctx:
        def sb(name, shape, dt=F32):
            return ctx.enter_context(nc.sbuf_tensor(f"dp_{name}", shape, dt))

        def ps(name, shape):
            return ctx.enter_context(nc.psum_tensor(f"dp_{name}", shape, F32))

        def sem(name):
            return ctx.enter_context(nc.semaphore(f"dp_{name}"))

        ident = sb("ident", [P, P])
        rel = sb("rel", [BUCKETS + 1, 2 * GROUPS])
        rel_b = sb("rel_b", [BUCKETS + 1, 2 * GROUPS, P])
        onehot = sb("onehot", [BUCKETS + 1, GROUPS, BIAS_ROW])
        by_dist = sb("by_dist", [P, 2 * GROUPS, BIAS_ROW])
        bias = sb("bias", [P, 2 * GROUPS, 2 * P])
        raw = sb("raw", [P, U, 3, P])
        qT = sb("qT", [P, U, P])
        kT = sb("kT", [P, U + 1, P])
        v_last = sb("v_last", [P, P])
        s_sb = sb("s_sb", [P, U, 2, 2 * P])
        probs = sb("probs", [P, U, 2, 2 * P])
        pT = sb("pT", [P, U, 2, 2, P])
        out = sb("out", [P, U, P + 4])
        neg = sb("neg", [P, U, 2])
        pause = sb("pause", [P, U])
        w_ps = ps("w", [P, U, 2, 512])

        setup, rel_ready, dist_mm, dist_ready, dist_stored, bias_landed = (sem(n) for n in (
            "setup", "rel_ready", "dist_mm", "dist_ready", "dist_stored", "bias_landed"))
        turned = sem("turned")
        qT_ready = sem("qT_ready")
        kT_ready = sem("kT_ready")
        scored = sem("scored")
        max_ready = sem("max_ready")
        exped = sem("exped")
        p_turned = sem("p_turned")
        pT_ready = sem("pT_ready")
        pv = sem("pv")
        o_ready = sem("o_ready")
        carried = sem("carried")
        stored = [sem(f"stored{u}") for u in range(U)]
        dve = Steps(sem("dve"))
        block = ctx.enter_context(nc.Block())

        prompt = pa[P:, :]
        out_rows = ma[P:, :]
        views = [lambda x: x.rearrange("(i u p) c -> i u p c", u=U, p=P),
                 lambda x: x.rearrange("(u p i) c -> i u p c", u=U, i=4),
                 lambda x: x.rearrange("(p i u) c -> i u p c", i=4, u=U)]

        def over_trips(eng, body, steps=None, per=0):
            def run(g, lo, hi, before):
                with eng.Fori(lo, hi) as i:
                    if steps:
                        with steps.loop(i - lo, hi - lo, per):
                            body(g, i, i + 4 * g, before)
                    else:
                        body(g, i, i + 4 * g, before)
            body(0, 0, 0, (False, True, True, True))
            run(0, 1, 4, (True,) * 4)
            run(1, 0, 4, (False, True, True, True))
            run(2, 0, 4, (False,) * 4)

        def dram(view, i, u, cols):
            return view[bass.ds(i, 1), u, :, cols].rearrange("a p c -> (a p) c")

        @block.sync
        def _(sp):
            sp.dma_start(ident[:], consts_d[:, IDENT]).then_inc(setup, 16)
            sp.dma_start(rel[:], rel_d).then_inc(setup, 16)
            sp.dma_start(onehot[:], onehot_d).then_inc(setup, 16)
            sp.wait_ge(dist_ready, 2 * GROUPS)
            for gh in range(2 * GROUPS):
                sp.dma_start(toep_d[gh], by_dist[:, gh]).then_inc(dist_stored, 16)
            sp.wait_ge(dist_stored, 16 * 2 * GROUPS)
            for gh in range(2 * GROUPS):
                sp.dma_start(bias[:, gh], bass.AP(tensor=toep_d.tensor, offset=gh * P * BIAS_ROW + P - 1,
                                                  ap=[[BIAS_ROW - 1, P], [1, 2 * P]])).then_inc(bias_landed, 16)

        @block.gpsimd
        def _(pool):
            def body(g, i, trip, before):
                view = views[g](prompt[:, 0:3 * A_WIDTH])
                for u in range(U):
                    pool.wait_ge(pv, trip * U + min(u + 2, U))
                    if u == U - 1:
                        pool.wait_ge(carried, trip + 1)
                    src = view[bass.ds(i, 1), u].rearrange("a p (k c) -> (a p) k c", k=3)[:, :, g * P:(g + 1) * P]
                    pool.dma_start(raw[:, u], src).then_inc(raw_landed[u], 16)
            over_trips(pool, body)

        @block.scalar
        def _(act):
            for u in range(U):
                act.sem_inc(stored[u], 32)
            act.sem_inc(exped, U)
            act.sem_inc(o_ready, U)
            act.sem_inc(carried, 1)

            def body(g, i, trip, before):
                view = views[g](out_rows)
                for u in range(U):
                    act.wait_ge(turned, trip * U + u + 1)
                    act.wait_ge(scored, trip * U + u + 1)
                    act.activation(qT[:, u], w_ps[:, u, 0, 0:P], ACT.Copy, scale=SCALE).then_inc(qT_ready, 1)
                for u in range(U):
                    act.wait_ge(max_ready, trip * U + u + 1)
                    act.wait_ge(p_turned, trip * U + u + 1)
                    lo = 0 if before[u] else P
                    for h in range(2):
                        last = act.activation(probs[:, u, h, lo:], s_sb[:, u, h, lo:], ACT.Exp,
                                              bias=neg[:, u, h:h + 1], accum_out=out[:, u, P + 2 + h:P + 3 + h])
                    last.then_inc(exped, 1)
                for u in range(U):
                    act.wait_ge(pv, trip * U + U + u + 1)
                    act.activation(out[:, u, 0:P].rearrange("p (h e) -> p h e", h=2), w_ps[:, u, :, 2 * P:2 * P + HD], ACT.Copy).then_inc(o_ready, 1)
                    act.wait_ge(o_ready, trip * U + U + u + 1)
                    act.dma_start(dram(view, i, u, slice(g * P, (g + 1) * P)), out[:, u, 0:P]).then_inc(stored[u], 16)
                    act.dma_start(dram(view, i, u, slice(A_WIDTH + 4 * g, A_WIDTH + 4 * g + 4)), out[:, u, P:P + 4]
                                  ).then_inc(stored[u], 16)
                act.activation(kT[:, U], kT[:, U - 1], ACT.Copy)
                act.activation(v_last[:], raw[:, U - 1, 2], ACT.Copy).then_inc(carried, 1)
            over_trips(act, body)
            for u in range(U):
                act.wait_ge(stored[u], 32 * 13)

        @block.vector
        def _(v):
            v.wait_ge(setup, 48)
            v.tensor_copy(rel_b[:], rel[:].unsqueeze(2).to_broadcast([BUCKETS + 1, 2 * GROUPS, P])
                          ).then_inc(rel_ready, 1)
            for gh in range(2 * GROUPS):
                v.wait_ge(dist_mm, gh + 1)
                v.tensor_copy(by_dist[:, gh], w_ps[:, gh % U, 0, 0:BIAS_ROW]
                              ).then_inc(dist_ready, 1)
            v.wait_ge(bias_landed, 16 * 2 * GROUPS)
            v.sem_inc(pT_ready, U)

            def body(g, i, trip, before):
                for u in range(U):
                    v.wait_ge(turned, trip * U + u + 1)
                    v.wait_ge(scored, trip * U + u + 1)
                    if u == U - 1:
                        v.wait_ge(carried, trip + 1)
                    v.wait_ge(qT_ready, trip * U + u + 1)
                    v.tensor_copy(kT[:, u], w_ps[:, u, 0, P:2 * P]).then_inc(kT_ready, 1)
                for u in range(U):
                    v.wait_ge(scored, trip * U + U + u + 1)
                    v.wait_ge(exped, trip * U + u + 1)
                    v.wait_ge(stored[u], trip * 32 + 32)
                    v.memset(pause[:, u:u + 1], 0.0)
                    lo = 0 if before[u] else P
                    for h in range(2):
                        last = v.tensor_tensor_reduce(
                            out=s_sb[:, u, h, lo:], in0=w_ps[:, u, h, lo:2 * P], in1=bias[:, 2 * g + h, lo:], scale=1.0,
                            scalar=NEG, op0=ALU.add, op1=ALU.max, accum_out=out[:, u, P + h:P + h + 1])
                    dve.link(v, last)
                    v.tensor_scalar(neg[:, u], out[:, u, P:P + 2], -1.0, None, ALU.mult).then_inc(max_ready, 1)
                for u in range(U):
                    v.wait_ge(p_turned, trip * U + U + u + 1)
                    v.wait_ge(pv, trip * U + u + 1)
                    lo = 0 if before[u] else 1
                    v.tensor_copy(pT[:, u, :, lo:], w_ps[:, u, :, 0:2 * P].rearrange("p h (k n) -> p h k n", k=2)
                                  [:, :, lo:]).then_inc(pT_ready, 1)
            over_trips(v, body, dve, U)

        @block.tensor
        def _(pe):
            pe.wait_ge(rel_ready, 1)
            for gh in range(2 * GROUPS):
                if gh >= U:
                    pe.wait_ge(dist_ready, gh - U + 1)
                pe.matmul(w_ps[:, gh % U, 0, 0:BIAS_ROW], rel_b[:, gh],
                          onehot[:, gh // 2], start=True, stop=True).then_inc(dist_mm, 1)
            pe.wait_ge(dist_ready, 2 * GROUPS)
            pe.sem_inc(scored, U)
            pe.sem_inc(p_turned, U)
            pe.sem_inc(pv, U)

            def body(g, i, trip, before):
                for u in range(U):
                    pe.wait_ge(raw_landed[u], trip * 16 + 16)
                    pe.wait_ge(o_ready, trip * U + u + 1)
                    pe.transpose(w_ps[:, u, 0, 0:P], raw[:, u, 0], ident[:])
                    pe.transpose(w_ps[:, u, 0, P:2 * P], raw[:, u, 1], ident[:]).then_inc(turned, 1)
                for u in range(U):
                    pe.wait_ge(qT_ready, trip * U + u + 1)
                    pe.wait_ge(kT_ready, trip * U + u + 1)
                    for h in range(2):
                        hs = slice(h * HD, (h + 1) * HD)
                        if before[u]:
                            pe.matmul(w_ps[:, u, h, 0:P], qT[hs, u], kT[hs, U if u == 0 else u - 1],
                                      start=True, stop=True)
                        last = pe.matmul(w_ps[:, u, h, P:2 * P], qT[hs, u], kT[hs, u], start=True, stop=True)
                    last.then_inc(scored, 1)
                for u in range(U):
                    pe.wait_ge(exped, trip * U + U + u + 1)
                    pe.wait_ge(pT_ready, trip * U + u + 1)
                    for h in range(2):
                        for k in range(0 if before[u] else 1, 2):
                            last = pe.transpose(w_ps[:, u, h, k * P:(k + 1) * P], probs[:, u, h, k * P:(k + 1) * P], ident[:])
                    last.then_inc(p_turned, 1)
                    pe.wait_ge(pT_ready, trip * U + U + u + 1)
                    for h in range(2):
                        hs = slice(h * HD, (h + 1) * HD)
                        if before[u]:
                            pe.matmul(w_ps[:, u, h, 2 * P:2 * P + HD], pT[:, u, h, 0], v_last[:, hs] if u == 0 else raw[:, u - 1, 2, hs],
                                      start=True, stop=False)
                        last = pe.matmul(w_ps[:, u, h, 2 * P:2 * P + HD], pT[:, u, h, 1], raw[:, u, 2, hs],
                                         start=not before[u], stop=True)
                    last.then_inc(pv, 1)
            over_trips(pe, body)


MIX_C = C_INNER + 1


def ssd_prompt(nc, pb, consts_d, conv_d, heads_d, gates, mc, p_ssm_d, p_conv_d):
    CT = CONV_DIM // P
    XT = C_INNER // P
    H = C_HEADS
    HG = H // C_GROUPS
    with ExitStack() as ctx:
        def sb(name, shape, dt=F32):
            return ctx.enter_context(nc.sbuf_tensor(f"sp_{name}", shape, dt))

        def ps(name, shape):
            return ctx.enter_context(nc.psum_tensor(f"sp_{name}_ps", shape, F32))

        def sem(name):
            return ctx.enter_context(nc.semaphore(f"sp_{name}"))

        consts = sb("consts", [P, 6, P])
        taps = sb("taps", [P, CT, C_CONV + 1])
        heads = sb("heads", [P, 2, H])
        a = sb("a", [P, ALL_TILES, H])
        dt = sb("dt", [P, ALL_TILES, H])
        e_cum = sb("e_cum", [P, ALL_TILES, H])
        e_rest = sb("e_rest", [P, ALL_TILES, H])
        e_all = sb("e_all", [P, ALL_TILES, H])
        a_now = sb("a_now", [P, 2, 5, H])
        raw = sb("raw", [P, 2, CDT])
        xT = sb("xT", [P, 2, CT, C_CONV - 1 + P])
        conv = sb("conv", [P, CT, P])
        tanh = sb("tanh", [P, CT, P])
        sT = sb("sT", [P, 2, CT, P])
        z2 = sb("z2", [P, 2, C_INNER])
        z_tanh = sb("z_tanh", [P, C_INNER])
        xs = sb("xs", [P, H, HD])
        xd = sb("xd", [P, H, HD])
        xdd = sb("xdd", [P, H, HD])
        skip = sb("skip", [P, H, HD])
        b_tok = sb("b_tok", [P, C_GROUPS, C_STATE])
        a_mask = sb("a_mask", [P, H, P])
        decay = sb("decay", [P, H, P])
        cb = sb("cb", [P, C_GROUPS, P])
        mix = sb("mix", [P, H, P])
        state = sb("state", [P, 2, H, HD])
        y = sb("y", [P, 2, H, HD])
        y_out = sb("y_out", [P, 2, MIX_C])
        sq_junk = sb("sq_junk", [P, C_INNER])
        fin = sb("fin", [P, XT, P])
        in_ps = ps("in", [P, 2, 512])
        x_ps = ps("x", [P, 512])
        b_ps = ps("b", [P, 512])
        seg_ps = ps("seg", [P, 2, 512])
        y_ps = ps("y", [P, 512])
        cb_ps = ps("cb", [P, 512])

        setup, halves, gates_a, gates_mm, gates_tmp, gates_exp = (sem(n) for n in (
            "setup", "halves", "gates_a", "gates_mm", "gates_tmp", "gates_exp"))
        landed = [sem("landed0"), sem("landed1")]
        in_turned = sem("in_turned")
        in_ready = sem("in_ready")
        conv_ready = sem("conv_ready")
        tanh_ready = sem("tanh_ready")
        s_ready = sem("s_ready")
        z_ready = sem("z_ready")
        tok_turned = sem("tok_turned")
        tok_ready = sem("tok_ready")
        xd_ready = sem("xd_ready")
        mask_ready = sem("mask_ready")
        seg_done = sem("seg_done")
        decay_ready = sem("decay_ready")
        cb_done = sem("cb_done")
        cb_ready = sem("cb_ready")
        mix_ready = sem("mix_ready")
        y_done = sem("y_done")
        st_done = sem("st_done")
        y_ready = sem("y_ready")
        state_ready = sem("state_ready")
        now_ready = sem("now_ready")
        skip_ready = sem("skip_ready")
        squared = sem("squared")
        fin_turned = sem("fin_turned")
        fin_ready = sem("fin_ready")
        stored = [sem("stored0"), sem("stored1")]
        out_done = sem("out_done")
        dve = Steps(sem("dve"))
        block = ctx.enter_context(nc.Block())
        ident = consts[:, IDENT]
        tri = consts[:, TRI_LE]

        def over_chunks(eng, first, body, steps=None, per=0):
            first(1, 1, 1, 1)
            with eng.Fori(0, 7) as i:
                def pair():
                    body(i * 2 + 1, 1, i + 1, True)
                    body(i * 2 + 2, 0, i + 1, True)
                if steps:
                    with steps.loop(i, 7, per):
                        pair()
                else:
                    pair()
            body(15, 1, 8, True)
            body(16, 0, 8, False)


        @block.sync
        def _(sp):
            sp.dma_start(consts[:], consts_d).then_inc(setup, 16)
            sp.dma_start(taps[:], conv_d).then_inc(setup, 16)
            sp.dma_start(heads[:], heads_d.rearrange("(a k) h -> a k h", a=1).broadcast_to([P, 2, H])
                         ).then_inc(setup, 16)

            def load(t, slot, use, _=0):
                sp.dma_start(raw[:, slot], rows(pb[:, 0:CDT], t)).then_inc(landed[slot], 16)

            def body(t, slot, n, more):
                if more:
                    sp.wait_ge(in_turned, t)
                    sp.wait_ge(z_ready, t)
                    load(t + 1, 1 - slot, None)
            over_chunks(sp, load, body)
            sp.wait_ge(fin_ready, 1)
            sp.dma_start(p_ssm_d.rearrange("(t p) n -> p t n", p=P), fin[:]).then_inc(out_done, 16)
            sp.dma_start(p_conv_d, xT[:, 0, :, P:P + C_CONV - 1]).then_inc(out_done, 16)
            sp.wait_ge(out_done, 32)

        @block.gpsimd
        def _(pool):
            pool.wait_ge(setup, 48)

            def body(t, slot, n, more):
                pool.wait_ge(now_ready, t)
                pool.wait_ge(seg_done, t)
                pool.tensor_tensor(a_mask[:], consts[:, TRI_GT].unsqueeze(1).to_broadcast([P, H, P]),
                                   a_now[:, slot, 1].unsqueeze(2).to_broadcast([P, H, P]), ALU.mult
                                   ).then_inc(mask_ready, 1)
                pool.wait_ge(xd_ready, t)
                pool.wait_ge(st_done, t)
                pool.tensor_tensor(xdd[:], xd[:], a_now[:, slot, 3].unsqueeze(2).to_broadcast([P, H, HD]), ALU.mult)
                pool.wait_ge(y_ready, t)
                pool.tensor_tensor(skip[:], xs[:], heads[:, 1].unsqueeze(2).to_broadcast([P, H, HD]), ALU.mult
                                   ).then_inc(skip_ready, 1)
                pool.wait_ge(decay_ready, t)
                pool.wait_ge(cb_ready, t + 1)
                pool.wait_ge(y_done, t)
                for g in range(C_GROUPS):
                    last = pool.tensor_tensor(mix[:, g * HG:(g + 1) * HG], decay[:, g * HG:(g + 1) * HG],
                                              cb[:, g].unsqueeze(1).to_broadcast([P, HG, P]), ALU.mult)
                last.then_inc(mix_ready, 1)
            over_chunks(pool, lambda *x: None, body)

        @block.scalar
        def _(act):
            act.wait_ge(gates_tmp, 1)
            act.activation(heads[:, 0], heads[:, 0], ACT.Exp).then_inc(gates_exp, 1)
            act.wait_ge(gates_mm, 1)
            act.activation(e_cum[:].rearrange("p t h -> p (t h)"), y_ps[:, 0:ALL_TILES * H], ACT.Exp)
            act.activation(e_all[:].rearrange("p t h -> p (t h)"), cb_ps[:, 0:ALL_TILES * H], ACT.Exp
                           ).then_inc(gates_exp, 1)
            act.wait_ge(gates_tmp, 2)
            act.activation(e_rest[:], e_rest[:], ACT.Exp).then_inc(gates_exp, 1)
            act.sem_inc(stored[0], 16)
            act.sem_inc(stored[1], 16)

            def ahead(t, slot, use, _=0):
                act.wait_ge(in_turned, t + 1)
                act.wait_ge(conv_ready, t)
                for b in range(2):
                    lo, hi = 4 * b, min(4 * b + 4, CT)
                    last = act.activation(xT[:, slot, lo:hi, C_CONV - 1:], in_ps[:, b, 0:(hi - lo) * P].rearrange(
                        "p (c n) -> p c n", n=P), ACT.Copy)
                last.then_inc(in_ready, 1)
                act.activation(z_tanh[:], raw[:, slot, CZ:CX], ACT.Tanh, scale=0.5)
                act.wait_ge(conv_ready, t + 1)
                act.activation(tanh[:], conv[:], ACT.Tanh).then_inc(tanh_ready, 1)

            def body(t, slot, n, more):
                act.wait_ge(tok_turned, t)
                act.wait_ge(skip_ready, t)
                act.wait_ge(st_done, t)
                act.activation(xs[:].rearrange("p h e -> p (h e)"), x_ps[:, 0:C_INNER], ACT.Copy)
                act.activation(b_tok[:].rearrange("p g n -> p (g n)"), b_ps[:, 0:2 * P], ACT.Copy
                               ).then_inc(tok_ready, 1)
                act.wait_ge(seg_done, t + 1)
                act.wait_ge(mix_ready, t)
                for g in range(C_GROUPS):
                    last = act.activation(decay[:, g * HG:(g + 1) * HG].rearrange("p h n -> p (h n)"),
                                          seg_ps[:, g, 0:HG * P], ACT.Exp)
                last.then_inc(decay_ready, 1)
                if more:
                    act.wait_ge(s_ready, t)
                    ahead(t + 1, 1 - slot, None)
                act.wait_ge(y_ready, t + 1)
                act.wait_ge(squared, t)
                act.activation(sq_junk[:], y_out[:, slot, 0:C_INNER], ACT.Square,
                               accum_out=y_out[:, slot, C_INNER:MIX_C]).then_inc(squared, 1)
                act.wait_ge(squared, t + 1)
                act.dma_start(rows(mc, t), y_out[:, slot]).then_inc(stored[slot], 16)
            act.sem_inc(squared, 1)
            over_chunks(act, ahead, body)
            act.wait_ge(stored[0], 16 * 9)
            act.wait_ge(stored[1], 16 * 9)

        @block.vector
        def _(v):
            v.wait_ge(setup, 48)
            dve.link(v, v.tensor_scalar(taps[:], taps[:], 0.5, None, ALU.mult))
            dve.link(v, v.tensor_copy(dt[:], gates[:, :, B_HEADS:B_HEADS + H]))
            v.memset(state[:, 1], 0.0)
            v.memset(xT[:, 1, :, 0:C_CONV - 1], 0.0).then_inc(gates_tmp, 1)
            v.wait_ge(gates_exp, 1)
            dve.link(v, v.tensor_scalar(heads[:, 0], heads[:, 0], -1.0, None, ALU.mult))
            v.tensor_tensor(a[:], dt[:], heads[:, 0].unsqueeze(1).to_broadcast([P, ALL_TILES, H]), ALU.mult
                            ).then_inc(gates_a, 1)
            v.wait_ge(gates_exp, 2)
            flat = e_rest[:].rearrange("p t h -> p (t h)")
            dve.link(v, v.tensor_copy(flat, y_ps[:, 0:ALL_TILES * H]))
            v.scalar_tensor_tensor(out=flat, in0=flat, scalar=-1.0, in1=cb_ps[:, 0:ALL_TILES * H],
                                   op0=ALU.mult, op1=ALU.add).then_inc(gates_tmp, 1)
            v.wait_ge(gates_exp, 3)
            for s in (conv_ready, cb_ready, y_ready, skip_ready):
                v.sem_inc(s, 1)

            def now(t, slot):
                for k, src in enumerate((dt, a, e_cum, e_rest, e_all)):
                    last = v.tensor_copy(a_now[:, slot, k:k + 1], src[:, bass.ds(t, 1)])
                last.then_inc(now_ready, 1)

            def ahead(t, slot, use, _=0):
                v.wait_ge(in_ready, t)
                v.tensor_copy(xT[:, 1 - slot, :, 0:C_CONV - 1], xT[:, slot, :, P:])
                v.wait_ge(tanh_ready, t)
                if not (isinstance(t, int) and t == 1):
                    v.wait_ge(s_ready, t - 1)
                for c in range(CT):
                    last = v.tensor_scalar(conv[:, c], xT[:, slot, c, 0:P], taps[:, c, 0:1],
                                           taps[:, c, C_CONV:C_CONV + 1], ALU.mult, ALU.add)
                dve.link(v, last)
                for j in range(1, C_CONV):
                    for c in range(CT):
                        last = v.scalar_tensor_tensor(out=conv[:, c], in0=xT[:, slot, c, j:j + P],
                                                      scalar=taps[:, c, j:j + 1], in1=conv[:, c],
                                                      op0=ALU.mult, op1=ALU.add)
                    if j < C_CONV - 1:
                        dve.link(v, last)
                last.then_inc(conv_ready, 1)
                v.wait_ge(tanh_ready, t + 1)
                v.wait_ge(conv_ready, t + 1)
                v.scalar_tensor_tensor(out=z2[:, slot], in0=z_tanh[:], scalar=1.0, in1=raw[:, slot, CZ:CX],
                                       op0=ALU.add, op1=ALU.mult).then_inc(z_ready, 1)
                v.scalar_tensor_tensor(out=sT[:, slot], in0=tanh[:], scalar=1.0, in1=conv[:],
                                       op0=ALU.add, op1=ALU.mult).then_inc(s_ready, 1)

            def body(t, slot, n, more):
                v.wait_ge(squared, t)
                now(t, slot)
                v.wait_ge(now_ready, t)
                v.wait_ge(tok_ready, t)
                v.tensor_tensor(xd[:], x_ps[:, 0:C_INNER].rearrange("p (h e) -> p h e", e=HD),
                                a_now[:, slot, 0].unsqueeze(2).to_broadcast([P, H, HD]), ALU.mult
                                ).then_inc(xd_ready, 1)
                v.wait_ge(cb_done, t)
                v.wait_ge(mix_ready, t)
                v.tensor_tensor(cb[:], cb_ps[:, 0:2 * P].rearrange("p (g n) -> p g n", n=P),
                                tri.unsqueeze(1).to_broadcast([P, C_GROUPS, P]), ALU.mult).then_inc(cb_ready, 1)
                if more:
                    ahead(t + 1, 1 - slot, None)
                v.wait_ge(st_done, t + 1)
                dve.link(v, v.tensor_tensor(state[:, 1 - slot], state[:, slot],
                                            a_now[:, slot, 4].unsqueeze(2).to_broadcast([P, H, HD]), ALU.mult))
                v.tensor_tensor(state[:, 1 - slot], state[:, 1 - slot],
                                seg_ps[:, 1, 0:C_INNER].rearrange("p (h e) -> p h e", e=HD), ALU.add
                                ).then_inc(state_ready, 1)
                v.wait_ge(y_done, t + 1)
                dve.link(v, v.tensor_tensor(y[:, 0], seg_ps[:, 0, 0:C_INNER].rearrange("p (h e) -> p h e", e=HD),
                                            a_now[:, slot, 2].unsqueeze(2).to_broadcast([P, H, HD]), ALU.mult))
                dve.link(v, v.tensor_tensor(y[:, 1], y[:, 0], y_ps[:, 0:C_INNER].rearrange("p (h e) -> p h e", e=HD),
                                            ALU.add))
                v.wait_ge(skip_ready, t + 1)
                dve.link(v, v.tensor_tensor(y[:, 0], y[:, 1], skip[:], ALU.add))
                v.wait_ge(stored[slot], n * 16)
                v.scalar_tensor_tensor(out=y_out[:, slot, 0:C_INNER], in0=y[:, 0].rearrange("p h e -> p (h e)"),
                                       scalar=0.5, in1=z2[:, slot], op0=ALU.mult, op1=ALU.mult).then_inc(y_ready, 1)

            over_chunks(v, ahead, body, dve, 2 * (3 + 1 + 3))
            v.wait_ge(fin_turned, 1)
            v.tensor_copy(fin[:], x_ps[:, 0:C_INNER].rearrange("p (t n) -> p t n", n=P)).then_inc(fin_ready, 1)

        @block.tensor
        def _(pe):
            pe.wait_ge(gates_a, 1)
            af = a[:].rearrange("p t h -> p (t h)")
            n = ALL_TILES * H
            pe.matmul(y_ps[:, 0:n], tri, af, start=True, stop=True)
            pe.matmul(cb_ps[:, 0:n], consts[:, ONES], af, start=True, stop=True).then_inc(gates_mm, 1)
            pe.wait_ge(gates_exp, 3)
            pe.wait_ge(gates_tmp, 2)
            for s in (in_turned, z_ready, seg_done, st_done, y_done, mix_ready, tanh_ready):
                pe.sem_inc(s, 1)

            def ahead(t, slot, use, _=0):
                pe.wait_ge(landed[slot], use * 16)
                if not (isinstance(t, int) and t == 1):
                    pe.wait_ge(in_ready, t - 1)
                for c in range(CT):
                    last = pe.transpose(in_ps[:, c // 4, (c % 4) * P:(c % 4 + 1) * P],
                                        raw[:, slot, CX + c * P:CX + (c + 1) * P], ident)
                last.then_inc(in_turned, 1)

            def body(t, slot, n, more):
                pe.wait_ge(s_ready, t)
                pe.wait_ge(now_ready, t)
                for c in range(XT):
                    pe.transpose(x_ps[:, c * P:(c + 1) * P], sT[:, slot, c], ident)
                for g in range(C_GROUPS):
                    last = pe.transpose(b_ps[:, g * P:(g + 1) * P], sT[:, slot, XT + g], ident)
                last.then_inc(tok_turned, 1)
                pe.wait_ge(cb_ready, t)
                for g in range(C_GROUPS):
                    last = pe.matmul(cb_ps[:, g * P:(g + 1) * P], sT[:, slot, XT + g], sT[:, slot, XT + C_GROUPS + g],
                                     start=True, stop=True)
                last.then_inc(cb_done, 1)
                pe.wait_ge(mask_ready, t)
                pe.wait_ge(y_ready, t)
                for h in range(H):
                    last = pe.matmul(seg_ps[:, h // HG, (h % HG) * P:(h % HG + 1) * P], a_mask[:, h], tri,
                                     start=True, stop=True)
                last.then_inc(seg_done, 1)
                if more:
                    ahead(t + 1, 1 - slot, n + (1 if slot == 0 else 0))
                pe.wait_ge(skip_ready, t + 1)
                pe.wait_ge(decay_ready, t)
                for g in range(C_GROUPS):
                    last = pe.matmul(seg_ps[:, 1, g * HG * HD:(g + 1) * HG * HD], b_tok[:, g],
                                     xdd[:, g * HG:(g + 1) * HG].rearrange("p h e -> p (h e)"), start=True, stop=True)
                last.then_inc(st_done, 1)
                for g in range(C_GROUPS):
                    pe.matmul(seg_ps[:, 0, g * HG * HD:(g + 1) * HG * HD], sT[:, slot, XT + C_GROUPS + g],
                              state[:, slot, g * HG:(g + 1) * HG].rearrange("p h e -> p (h e)"), start=True, stop=True)
                pe.wait_ge(mix_ready, t + 1)
                for h in range(H):
                    last = pe.matmul(y_ps[:, h * HD:(h + 1) * HD], mix[:, h], xd[:, h], start=True, stop=True)
                last.then_inc(y_done, 1)
            over_chunks(pe, ahead, body)
            pe.wait_ge(state_ready, TILES)
            for c in range(XT):
                last = pe.transpose(x_ps[:, c * P:(c + 1) * P],
                                    state[:, 1, 2 * c:2 * c + 2].rearrange("p h e -> p (h e)"), ident)
            last.then_inc(fin_turned, 1)


def newton(v, dve, rstd, mean, root, tmp):
    dve.link(v, v.reciprocal(rstd, root))
    dve.link(v, v.tensor_tensor(tmp, rstd, rstd, ALU.mult))
    dve.link(v, v.tensor_tensor(tmp, tmp, mean, ALU.mult))
    dve.link(v, v.tensor_scalar(tmp, tmp, -0.5, 1.5, ALU.mult, ALU.add))
    return v.tensor_tensor(rstd, rstd, tmp, ALU.mult)


def over_pipeline(eng, body, steps=None, per=0):
    body(0, 0, 1, True, False)
    with eng.Fori(0, 7) as i:
        def pair():
            body(i * 2 + 1, 1, i + 1, False, False)
            body(i * 2 + 2, 0, i + 2, False, False)
        if steps:
            with steps.loop(i, 7, per):
                pair()
        else:
            pair()
    body(15, 1, 8, False, False)
    body(16, 0, 9, False, True)


def out_project(nc, ma, mb, mc, x_d, w_d, consts_d, norm_w_d, lnw_d, x2_d, h2_d):
    H2 = 2 * GROUPS
    with ExitStack() as ctx:
        def sb(name, shape, dt=F32):
            return ctx.enter_context(nc.sbuf_tensor(f"op_{name}", shape, dt))

        def ps(name, shape):
            return ctx.enter_context(nc.psum_tensor(f"op_{name}_ps", shape, F32))

        def sem(name):
            return ctx.enter_context(nc.semaphore(f"op_{name}"))

        ident = sb("ident", [P, P])
        norm_w = sb("norm_w", [P, C_INNER])
        lnw = sb("lnw", [P, KT])
        w_raw = sb("w_raw", [P, 2, D_MODEL])
        w_hi = sb("w_hi", [P, KT, D_MODEL], F32R)
        w_lo = sb("w_lo", [P, KT, D_MODEL], F32R)
        stats = sb("stats", [P, ALL_TILES, GROUPS, 4])
        top = sb("top", [P, ALL_TILES, 2])
        share = sb("share", [P, ALL_TILES, GROUPS, 2])
        whole = sb("whole", [P, ALL_TILES, 2])
        part = sb("part", [P, ALL_TILES, 2])
        c_sum = sb("c_sum", [P, ALL_TILES, 1])
        c_root = sb("c_root", [P, ALL_TILES, 1])
        c_tmp = sb("c_tmp", [P, ALL_TILES, 1])
        c_rstd = sb("c_rstd", [P, ALL_TILES, 1])
        mix = sb("mix", [P, 2, D_MODEL])
        x = sb("x", [P, 2, D_MODEL])
        share_now = sb("share_now", [P, 2, H2])
        c_now = sb("c_now", [P, 2])
        m_hi = sb("m_hi", [P, 2, KT, P], F32R)
        m_lo = sb("m_lo", [P, 2, KT, P], F32R)
        x2 = sb("x2", [P, 2, D_MODEL])
        xn = sb("xn", [P, D_MODEL])
        h2 = sb("h2", [P, 2, KT, P])
        sq = sb("sq", [P, 2])
        root = sb("root", [P, 2])
        rstd = sb("rstd", [P, 2])
        tmp = sb("tmp", [P, 2])
        in_ps = ps("in", [P, 2, 4, P])
        acc_ps = ps("acc", [P, 2, 2, 512])
        tr_ps = ps("tr", [P, 2, 4, P])

        setup, shares_exp, factors, c_mean, c_rooted = (sem(n) for n in (
            "setup", "shares_exp", "factors", "c_mean", "c_rooted"))
        w_landed = [sem(f"w_landed{k}") for k in range(2)]
        hi_ready, w_ready = sem("hi_ready"), sem("w_ready")
        landed = [sem(f"landed{k}") for k in range(2)]
        x_landed = [sem(f"x_landed{k}") for k in range(2)]
        mixed = sem("mixed")
        m_turned = sem("m_turned")
        m_hi_ready = sem("m_hi_ready")
        m_ready = sem("m_ready")
        mm_done = sem("mm_done")
        x2_ready = sem("x2_ready")
        squared = sem("squared")
        mean_ready = sem("mean_ready")
        rooted = sem("rooted")
        rstd_ready = sem("rstd_ready")
        xn_ready = sem("xn_ready")
        turned = sem("turned")
        h2_ready = sem("h2_ready")
        x2_stored = [sem(f"x2_stored{k}") for k in range(2)]
        h2_stored = [sem(f"h2_stored{k}") for k in range(2)]
        dve = Steps(sem("dve"))
        pool_steps = Steps(sem("pool"))
        block = ctx.enter_context(nc.Block())

        @block.sync
        def _(sp):
            sp.dma_start(stats[:].rearrange("p t g k -> p t (g k)"),
                         ma[:, A_WIDTH:MIX_A].rearrange("(t p) c -> p t c", p=P)).then_inc(setup, 16)
            sp.dma_start(c_sum[:], mc[:, C_INNER:MIX_C].rearrange("(t p) c -> p t c", p=P), allow_slow_non_contiguous=True).then_inc(setup, 16)
            sp.dma_start(ident[:], consts_d[:, IDENT]).then_inc(setup, 16)
            sp.dma_start(norm_w[:], norm_w_d.rearrange("(a n) -> a n", a=1).broadcast_to([P, C_INNER])
                         ).then_inc(setup, 16)
            sp.dma_start(lnw[:], lnw_d).then_inc(setup, 16)

            def load(t, slot):
                sp.dma_start(mix[:, slot, 0:A_WIDTH], rows(ma[:, 0:A_WIDTH], t)).then_inc(landed[slot], 16)
                sp.dma_start(mix[:, slot, A_WIDTH:A_WIDTH + B_WIDTH], rows(mb, t)).then_inc(landed[slot], 16)
                sp.dma_start(mix[:, slot, A_WIDTH + B_WIDTH:], rows(mc[:, 0:C_INNER], t)).then_inc(landed[slot], 16)

            def load_x(t, slot):
                sp.dma_start(x[:, slot], rows(x_d, t)).then_inc(x_landed[slot], 16)

            load(0, 0)
            load_x(0, 0)
            for k in range(KT):
                if k >= 2:
                    sp.wait_ge(w_ready, k - 1)
                sp.dma_start(w_raw[:, k % 2], w_d[:, k]).then_inc(w_landed[k % 2], 16)

            def body(t, slot, use, first, last):
                if not last:
                    sp.wait_ge(m_turned, t + 1)
                    load(t + 1, 1 - slot)
                    sp.wait_ge(x2_ready, t + 1)
                    load_x(t + 1, 1 - slot)
            sp.sem_inc(m_turned, 1)
            over_pipeline(sp, body)

        @block.gpsimd
        def _(pool):
            pool.wait_ge(factors, 2)

            def body(t, slot, use, first, last):
                pool.wait_ge(landed[slot], use * 48)
                if not first:
                    pool.wait_ge(mixed, t)
                pool_steps.mark(pool.tensor_copy(share_now[:, slot:slot + 1],
                                                 share[:].rearrange("p t g h -> p t (g h)")[:, bass.ds(t, 1)]))
                pool_steps.link(pool, pool.tensor_copy(c_now[:, slot:slot + 1], c_rstd[:, bass.ds(t, 1), 0]))
                c = mix[:, slot, A_WIDTH + B_WIDTH:]
                pool_steps.link(pool, pool.tensor_tensor(c, c, c_now[:, slot:slot + 1].to_broadcast([P, C_INNER]), ALU.mult))
                pool.tensor_tensor(mix[:, slot, A_WIDTH + B_WIDTH:], mix[:, slot, A_WIDTH + B_WIDTH:], norm_w[:],
                                   ALU.mult)
                m = mix[:, slot, 0:A_WIDTH].rearrange("p (g e) -> p g e", e=HD)
                pool.tensor_tensor(m, m, share_now[:, slot].unsqueeze(2).to_broadcast([P, H2, HD]), ALU.mult
                                   ).then_inc(mixed, 1)
            over_pipeline(pool, body, pool_steps, 6)

        @block.scalar
        def _(act):
            act.wait_ge(shares_exp, 1)
            act.activation(share[:], share[:], ACT.Exp).then_inc(shares_exp, 1)
            for k in range(KT):
                act.wait_ge(w_landed[k % 2], 16 * (k // 2 + 1))
                act.activation(w_hi[:, k], w_raw[:, k % 2], ACT.Copy).then_inc(hi_ready, 1)
            act.wait_ge(c_mean, 1)
            act.activation(c_root[:], c_sum[:], ACT.Sqrt).then_inc(c_rooted, 1)
            act.sem_inc(h2_stored[0], 16)
            act.sem_inc(h2_stored[1], 16)
            act.sem_inc(rooted, 1)
            act.sem_inc(xn_ready, 1)

            def split(t, slot):
                act.wait_ge(m_turned, t + 2)
                if not (isinstance(t, int) and t == 0):
                    act.wait_ge(mm_done, t)
                act.activation(m_hi[:, slot].rearrange("p (a b) n -> p a b n", a=2), in_ps[:], ACT.Copy
                               ).then_inc(m_hi_ready, 1)

            def norm(t, slot):
                act.wait_ge(x2_ready, t + 2)
                act.wait_ge(turned, t + 1)
                act.dma_start(rows(x2_d, t), x2[:, slot]).then_inc(x2_stored[slot], 16)
                act.activation(xn[:], x2[:, slot], ACT.Square, accum_out=sq[:, slot:slot + 1]).then_inc(squared, 1)
                act.wait_ge(mean_ready, t + 1)
                act.activation(root[:, slot:slot + 1], sq[:, slot:slot + 1], ACT.Sqrt).then_inc(rooted, 1)
                act.wait_ge(rstd_ready, t + 1)
                act.activation(xn[:], x2[:, slot], ACT.Copy, scale=rstd[:, slot:slot + 1]).then_inc(xn_ready, 1)

            def store(t, slot):
                act.wait_ge(h2_ready, t + 2)
                act.dma_start(h2_d[bass.ds(t, 1)].rearrange("a p k n -> (a p) k n"), h2[:, slot]
                              ).then_inc(h2_stored[slot], 16)

            split(0, 0)

            def body(t, slot, use, first, last):
                if not last:
                    split(t + 1, 1 - slot)
                if not first:
                    norm(t - 1, 1 - slot)
                    store(t - 1, 1 - slot)
            over_pipeline(act, body)
            norm(16, 0)
            store(16, 0)
            act.wait_ge(x2_stored[0], 16 * 10)
            act.wait_ge(x2_stored[1], 16 * 9)
            act.wait_ge(h2_stored[0], 16 * 10)
            act.wait_ge(h2_stored[1], 16 * 9)

        @block.vector
        def _(v):
            v.sem_inc(x2_ready, 1)
            v.sem_inc(h2_ready, 1)
            v.sem_inc(x2_stored[1], 16)
            v.sem_inc(x2_stored[0], 16)
            v.wait_ge(setup, 80)
            big = [stats[:, :, g, 0:2] for g in range(GROUPS)]
            dve.link(v, v.tensor_tensor(top[:], big[0], big[1], ALU.max))
            dve.link(v, v.tensor_tensor(top[:], top[:], big[2], ALU.max))
            v.tensor_tensor(share[:], stats[:, :, :, 0:2], top[:].unsqueeze(2).to_broadcast(
                [P, ALL_TILES, GROUPS, 2]), ALU.subtract).then_inc(shares_exp, 1)
            v.wait_ge(shares_exp, 2)
            dve.link(v, v.tensor_tensor(whole[:], share[:, :, 0], stats[:, :, 0, 2:4], ALU.mult))
            for g in range(1, GROUPS):
                dve.link(v, v.tensor_tensor(part[:], share[:, :, g], stats[:, :, g, 2:4], ALU.mult))
                dve.link(v, v.tensor_tensor(whole[:], whole[:], part[:], ALU.add))
            dve.link(v, v.reciprocal(whole[:], whole[:]))
            v.tensor_tensor(share[:], share[:], whole[:].unsqueeze(2).to_broadcast([P, ALL_TILES, GROUPS, 2]),
                            ALU.mult).then_inc(factors, 1)
            v.tensor_scalar(c_sum[:], c_sum[:], 1.0 / C_INNER, EPS, ALU.mult, ALU.add).then_inc(c_mean, 1)
            for k in range(KT):
                v.wait_ge(hi_ready, k + 1)
                v.tensor_tensor(w_lo[:, k], w_raw[:, k % 2], w_hi[:, k].bitcast(F32), ALU.subtract
                                ).then_inc(w_ready, 1)
            v.wait_ge(c_mean, 1)
            v.wait_ge(c_rooted, 1)
            newton(v, dve, c_rstd[:], c_sum[:], c_root[:], c_tmp[:]).then_inc(factors, 1)

            def split(t, slot):
                v.wait_ge(m_hi_ready, t + 1)
                v.tensor_tensor(m_lo[:, slot].rearrange("p (a b) n -> p a b n", a=2), in_ps[:],
                                m_hi[:, slot].rearrange("p (a b) n -> p a b n", a=2).bitcast(F32), ALU.subtract
                                ).then_inc(m_ready, 1)

            def residual(t, slot):
                v.wait_ge(mm_done, t + 2)
                v.wait_ge(xn_ready, t + 1)
                v.wait_ge(x2_stored[slot], use_now[0] * 16)
                v.wait_ge(x_landed[slot], use_now[0] * 16)
                v.tensor_tensor(x2[:, slot], acc_ps[:, slot].rearrange("p a n -> p (a n)"), x[:, slot], ALU.add
                                ).then_inc(x2_ready, 1)
                v.wait_ge(squared, t + 1)
                dve.link(v, v.tensor_scalar(sq[:, slot:slot + 1], sq[:, slot:slot + 1], 1.0 / D_MODEL, EPS,
                                            ALU.mult, ALU.add))
                v.tensor_copy(tmp[:, 1:2], sq[:, slot:slot + 1]).then_inc(mean_ready, 1)
                v.wait_ge(mean_ready, t + 1)
                v.wait_ge(rooted, t + 2)
                newton(v, dve, rstd[:, slot:slot + 1], tmp[:, 1:2], root[:, slot:slot + 1], tmp[:, 0:1]
                       ).then_inc(rstd_ready, 1)

            def weigh(t, slot):
                v.wait_ge(turned, t + 2)
                v.wait_ge(h2_stored[slot], use_now[0] * 16)
                v.tensor_tensor(h2[:, slot].rearrange("p (a b) n -> p a b n", a=2), tr_ps[:],
                                lnw[:].rearrange("p (a b) -> p a b", a=2).unsqueeze(3).to_broadcast([P, 2, 4, P]),
                                ALU.mult).then_inc(h2_ready, 1)

            use_now = [None]
            split(0, 0)

            def body(t, slot, use, first, last):
                if not last:
                    split(t + 1, 1 - slot)
                if not first:
                    use_now[0] = use - 1 if slot == 0 else use
                    residual(t - 1, 1 - slot)
                    weigh(t - 1, 1 - slot)
            over_pipeline(v, body, dve, 2 * 5)
            use_now[0] = 9
            residual(16, 0)
            weigh(16, 0)

        @block.tensor
        def _(pe):
            pe.sem_inc(turned, 1)
            pe.sem_inc(mm_done, 1)

            def turn_in(t, slot):
                pe.wait_ge(mixed, t + 1)
                if not (isinstance(t, int) and t == 0):
                    pe.wait_ge(m_ready, t)
                for k in range(KT):
                    last = pe.transpose(in_ps[:, k // 4, k % 4], mix[:, slot, k * P:(k + 1) * P], ident[:])
                last.then_inc(m_turned, 1)

            def turn_out(t):
                pe.wait_ge(xn_ready, t + 2)
                pe.wait_ge(h2_ready, t + 1)
                for k in range(KT):
                    last = pe.transpose(tr_ps[:, k // 4, k % 4], xn[:, k * P:(k + 1) * P], ident[:])
                last.then_inc(turned, 1)

            turn_in(0, 0)
            pe.wait_ge(w_ready, KT)

            def body(t, slot, use, first, last):
                if not last:
                    turn_in(t + 1, 1 - slot)
                pe.wait_ge(m_ready, t + 1)
                if not first:
                    pe.wait_ge(x2_ready, t)
                for b in range(2):
                    cs = slice(b * 512, (b + 1) * 512)
                    for k in range(KT):
                        pe.matmul(acc_ps[:, slot, b], m_hi[:, slot, k], w_hi[:, k, cs], start=(k == 0), stop=False)
                        pe.matmul(acc_ps[:, slot, b], m_hi[:, slot, k], w_lo[:, k, cs], start=False, stop=False)
                        mm = pe.matmul(acc_ps[:, slot, b], m_lo[:, slot, k], w_hi[:, k, cs], start=False,
                                       stop=(k == KT - 1))
                mm.then_inc(mm_done, 1)
                if not first:
                    turn_out(t - 1)
            over_pipeline(pe, body)
            turn_out(16)


def channel_mixer(nc, tag, sample, first_tile, h2_d, x2_d, w_up_d, w_down_d, small_d, final_w_d,
                  edge, y_p_d, y_s_d, s_gate_d):
    TT = TILES // 2
    NT = TT * P + (DEC if sample else 0)
    widths = [344] * 3 if sample else [512] * 2
    nb = len(widths)
    at = [sum(widths[:b]) for b in range(nb + 1)]
    assert at[nb] == NT
    YT = TT + (1 if sample else 0)
    NA = YT * P
    W = widths[0]
    HALO = FFN_CONV - 1
    TRIPS = FF_TILES // 2
    with ExitStack() as ctx:
        def sb(name, shape, dt=F32):
            return ctx.enter_context(nc.sbuf_tensor(f"{tag}_{name}", shape, dt))

        def ps(name, shape):
            return ctx.enter_context(nc.psum_tensor(f"{tag}_{name}_ps", shape, F32))

        def sem(name):
            return ctx.enter_context(nc.semaphore(f"{tag}_{name}"))

        h_hi = sb("h_hi", [P, KT, NT], F32R)
        h_lo = sb("h_lo", [P, KT, NT], F32R)
        y = sb("y", [P, YT, D_MODEL])
        up_raw = sb("up_raw", [P, 2, KT, 2 * P])
        up_hi = sb("up_hi", [P, 2, KT, 2 * P], F32R)
        up_lo = sb("up_lo", [P, 2, KT, 2 * P], F32R)
        dn_raw = sb("dn_raw", [P, 2, D_MODEL])
        dn_hi = sb("dn_hi", [P, 2, D_MODEL], F32R)
        dn_lo = sb("dn_lo", [P, 2, D_MODEL], F32R)
        small = sb("small", [P, 2, FFN_CONV + 1 + HALO * DEC])
        gate = sb("gate", [P, 2, HALO + NT])
        conv = sb("conv", [P, W])
        a_hi = sb("a_hi", [P, 2, NA], F32R)
        a_lo = sb("a_lo", [P, 2, NA], F32R)
        s_gate = sb("s_gate", [P, FF_TILES, DEC])
        sq = sb("sq", [P, YT])
        root = sb("root", [P, YT])
        tmp = sb("tmp", [P, YT])
        rstd = sb("rstd", [P, YT])
        g_ps = ps("g", [P, nb, 512])
        u_ps = ps("u", [P, nb, 512])
        y_ps = ps("y", [P, 2, 512])

        setup = sem("setup")
        y_landed = sem("y_landed")
        h_landed = [sem(f"h_landed{k}") for k in range(2)]
        h_hi_ready, h_ready = sem("h_hi_ready"), sem("h_ready")
        up_landed = [sem(f"up_landed{k}") for k in range(2)]
        small_landed = [sem(f"small_landed{k}") for k in range(2)]
        dn_landed = [sem(f"dn_landed{k}") for k in range(2)]
        up_hi_ready, up_ready = sem("up_hi_ready"), sem("up_ready")
        dn_hi_ready, dn_ready = sem("dn_hi_ready"), sem("dn_ready")
        gated = sem("gated")
        gate_ready = sem("gate_ready")
        upped = sem("upped")
        conv_ready = sem("conv_ready")
        act_ready = sem("act_ready")
        a_hi_ready, a_ready = sem("a_hi_ready"), sem("a_ready")
        prod_ready = sem("prod_ready")
        downed = sem("downed")
        added = sem("added")
        squared, mean_ready, rooted, y_done, stored = (sem(n) for n in (
            "squared", "mean_ready", "rooted", "y_done", "stored"))
        dve = Steps(sem("dve"))
        block = ctx.enter_context(nc.Block())
        def sums(n):
            return y_ps[:] if n % 2 == 0 else g_ps[:, 0:2]

        stage = dn_raw[:].rearrange("p s (k n) -> p s k n", k=KT)
        tiles = [(first_tile + i, i * P, P) for i in range(TT)] + ([(0, TT * P, DEC)] if sample else [])

        def over_trips(eng, body, steps=None, per=0):
            with eng.Fori(0, TRIPS) as i:
                if steps:
                    with steps.loop(i, TRIPS, per):
                        body(i)
                else:
                    body(i)

        @block.sync
        def _(sp):
            def weights_up(i, s):
                sp.dma_start(up_raw[:, s], w_up_d[bass.ds(i * 2 + s, 1)].rearrange("a p k n -> (a p) k n")
                             ).then_inc(up_landed[s], 16)

            def load_h(n, t):
                sp.dma_start(stage[:, n % 2], h2_d[t]).then_inc(h_landed[n % 2], 16)

            load_h(0, tiles[0][0])
            load_h(1, tiles[1][0])
            sp.dma_start(up_raw[:, 0], w_up_d[0]).then_inc(up_landed[0], 16)
            sp.dma_start(up_raw[:, 1], w_up_d[1]).then_inc(up_landed[1], 16)
            for n, (t, _, _) in enumerate(tiles):
                if n >= 2:
                    sp.wait_ge(h_ready, n - 1)
                    load_h(n, t)
            sp.wait_ge(h_ready, len(tiles))

            def body(i):
                for s in range(2):
                    sp.wait_ge(conv_ready, (i * 2 + s + 1) * nb)
                    sp.dma_start(small[:, s], small_d[bass.ds(i * 2 + s, 1)].rearrange("a p n -> (a p) n")
                                 ).then_inc(small_landed[s], 16)
                for s in range(2):
                    sp.wait_ge(dn_ready, i * 2 + s + 1)
                    sp.dma_start(dn_raw[:, s], w_down_d[bass.ds((i * 2 + s) * P, P), :]).then_inc(dn_landed[s], 16)

            def ahead(i):
                for s in range(2):
                    sp.wait_ge(up_ready, i * 2 + s + 3)
                    weights_up(i + 1, s)

            with sp.Fori(0, TRIPS - 1) as i:
                body(i)
                ahead(i)
            body(TRIPS - 1)
            sp.wait_ge(dn_ready, FF_TILES + 1)
            sp.dma_start(dn_raw[:, 0], final_w_d.rearrange("(a n) -> a n", a=1).broadcast_to([P, D_MODEL])
                         ).then_inc(y_landed, 16)

        @block.gpsimd
        def _(pool):
            pool.memset(a_hi[:, :, NT:].bitcast(F32), 0.0) if sample else None
            pool.memset(a_lo[:, :, NT:].bitcast(F32), 0.0).then_inc(setup, 1) if sample else pool.sem_inc(setup, 1)
            pool.sem_inc(up_ready, 2)
            pool.sem_inc(dn_ready, 2)

            def body(i):
                for s in range(2):
                    pool.wait_ge(up_hi_ready, i * 2 + s + 1)
                    pool.wait_ge(upped, (i * 2 + s + 1) * nb)
                    pool.tensor_tensor(up_lo[:, s], up_raw[:, s], up_hi[:, s].bitcast(F32), ALU.subtract
                                       ).then_inc(up_ready, 1)
                for s in range(2):
                    pool.wait_ge(dn_hi_ready, i * 2 + s + 1)
                    pool.wait_ge(downed, i * YT + 1)
                    pool.tensor_tensor(dn_lo[:, s], dn_raw[:, s], dn_hi[:, s].bitcast(F32), ALU.subtract
                                       ).then_inc(dn_ready, 1)
            over_trips(pool, body)

        @block.scalar
        def _(act):
            for n, (t, c, w) in enumerate(tiles):
                act.wait_ge(h_landed[n % 2], 16 * (n // 2 + 1))
                act.activation(h_hi[:, :, c:c + w], stage[:, n % 2, :, 0:w], ACT.Copy).then_inc(h_hi_ready, 1)

            for n, (t, c, w) in enumerate(tiles):
                act.dma_start(y[:, n], x2_d[t * P:(t + 1) * P, :]).then_inc(y_landed, 16)
            act.sem_inc(gate_ready, nb)
            act.sem_inc(act_ready, 1)

            def body(i):
                for s in range(2):
                    act.wait_ge(up_landed[s], i * 16 + 16)
                    act.wait_ge(upped, (i * 2 + s + 1) * nb)
                    act.activation(up_hi[:, s], up_raw[:, s], ACT.Copy).then_inc(up_hi_ready, 1)
                for s in range(2):
                    n0 = (i * 2 + s) * nb
                    for b in range(nb):
                        act.wait_ge(gated, n0 + b + 1)
                        act.wait_ge(prod_ready, n0 + nb)
                        act.activation(gate[:, s, HALO + at[b]:HALO + at[b + 1]], g_ps[:, b, 0:widths[b]], ACT.Copy
                                       ).then_inc(gate_ready, 1)
                    for b in range(nb):
                        act.wait_ge(conv_ready, n0 + 2 * nb + b + 1)
                        act.activation(gate[:, s, at[b]:at[b + 1]], conv[:, 0:widths[b]], ACT.Silu
                                       ).then_inc(act_ready, 1)
                for s in range(2):
                    act.wait_ge(dn_landed[s], i * 16 + 16)
                    act.wait_ge(downed, i * YT + 1)
                    act.activation(dn_hi[:, s], dn_raw[:, s], ACT.Copy).then_inc(dn_hi_ready, 1)
            over_trips(act, body)
            act.wait_ge(added, TRIPS * YT + 2)
            for n in range(YT):
                act.activation(gate[:, 0, 0:D_MODEL], y[:, n], ACT.Square, accum_out=sq[:, n:n + 1]).then_inc(squared, 1)
                act.wait_ge(squared, n + 1)
            act.wait_ge(mean_ready, 1)
            act.activation(root[:], sq[:], ACT.Sqrt).then_inc(rooted, 1)
            for n, (t, c, w) in enumerate(tiles):
                act.wait_ge(y_done, n + 1)
                dst = y_s_d if t == 0 else y_p_d[(t - 1) * P:t * P, :]
                act.dma_start(dst, y[0:w, n]).then_inc(stored, 16)
            if sample:
                act.dma_start(s_gate_d, s_gate[:]).then_inc(stored, 16)
            act.wait_ge(stored, 16 * (YT + (1 if sample else 0)))

        @block.vector
        def _(v):
            for n, (t, c, w) in enumerate(tiles):
                v.wait_ge(h_hi_ready, n + 1)
                v.tensor_tensor(h_lo[:, :, c:c + w], stage[:, n % 2, :, 0:w], h_hi[:, :, c:c + w].bitcast(F32),
                                ALU.subtract).then_inc(h_ready, 1)
            if sample:
                v.memset(edge[:], 0.0).then_inc(setup, 1)
            else:
                v.sem_inc(setup, 1)
            v.wait_ge(setup, 2)
            v.sem_inc(prod_ready, 2 * nb)
            v.sem_inc(conv_ready, 2 * nb)
            v.sem_inc(added, 2)

            def convolve(i, s):
                n0 = (i * 2 + s) * nb
                taps = [small[:, s, k:k + 1] for k in range(FFN_CONV)]
                tap_b = small[:, s, FFN_CONV:FFN_CONV + 1]
                before = [small[:, s, FFN_CONV + 1 + k * DEC:FFN_CONV + 1 + (k + 1) * DEC] for k in range(HALO)]
                v.wait_ge(small_landed[s], i * 16 + 16)
                v.wait_ge(prod_ready, n0 + nb)
                dve.link(v, v.tensor_copy(gate[:, s, 0:HALO], edge[:, bass.ds(i * 2 + s, 1)].rearrange("p a n -> p (a n)")))
                for b in range(nb):
                    w = widths[b]
                    ws = w - DEC if sample and b == nb - 1 else w
                    v.wait_ge(gate_ready, n0 + nb + b + 1)
                    v.wait_ge(act_ready, n0 + b + 1)
                    dve.link(v, v.tensor_scalar(conv[:, 0:ws], gate[:, s, at[b]:at[b] + ws], taps[0], tap_b,
                                                ALU.mult, ALU.add))
                    if ws != w:
                        dve.link(v, v.tensor_scalar(conv[:, ws:w], before[0], taps[0], tap_b, ALU.mult, ALU.add))
                    for k in range(1, FFN_CONV):
                        last = v.scalar_tensor_tensor(out=conv[:, 0:ws], in0=gate[:, s, at[b] + k:at[b] + k + ws],
                                                      scalar=taps[k], in1=conv[:, 0:ws], op0=ALU.mult, op1=ALU.add)
                        if ws != w:
                            src = before[k] if k < HALO else gate[:, s, HALO + NT - DEC:HALO + NT]
                            last = v.scalar_tensor_tensor(out=conv[:, ws:w], in0=src, scalar=taps[k],
                                                          in1=conv[:, ws:w], op0=ALU.mult, op1=ALU.add)
                        if k == 1 and b == nb - 1:
                            end = at[nb] - (DEC if sample else 0)
                            v.tensor_copy(edge[:, bass.ds(i * 2 + s, 1)].rearrange("p a n -> p (a n)"),
                                          gate[:, s, end:end + HALO])
                            if sample:
                                v.tensor_copy(s_gate[:, bass.ds(i * 2 + s, 1)].rearrange("p a n -> p (a n)"),
                                              gate[:, s, HALO + NT - DEC:HALO + NT])
                        if k < FFN_CONV - 1:
                            dve.link(v, last)
                    last.then_inc(conv_ready, 1)

            def multiply(i, s):
                n0 = (i * 2 + s) * nb
                for b in range(nb):
                    w = widths[b]
                    v.wait_ge(act_ready, n0 + b + 2)
                    v.wait_ge(upped, n0 + 2 * nb + b + 1)
                    if b == 0:
                        v.wait_ge(downed, i * YT + 1)
                    cs = slice(at[b], at[b + 1])
                    g = gate[:, s, at[b]:at[b + 1]]
                    dve.link(v, v.tensor_tensor(g, g, u_ps[:, b, 0:w], ALU.mult))
                    dve.link(v, v.tensor_copy(a_hi[:, s, cs], g))
                    v.tensor_tensor(a_lo[:, s, cs], g, a_hi[:, s, cs].bitcast(F32), ALU.subtract
                                    ).then_inc(prod_ready, 1)

            def body(i):
                convolve(i, 0)
                convolve(i, 1)
                multiply(i, 0)
                multiply(i, 1)
                v.wait_ge(y_landed, 16 * YT)
                for n in range(YT):
                    v.wait_ge(downed, i * YT + n + 2)
                    v.tensor_tensor(y[:, n], y[:, n], sums(n).rearrange("p a n -> p (a n)"), ALU.add
                                    ).then_inc(added, 1)

            over_trips(v, body, dve, 2 * (1 + nb * 4 + (1 if sample else 0)))
            v.wait_ge(squared, YT)
            dve.link(v, v.tensor_scalar(sq[:], sq[:], 1.0 / D_MODEL, EPS, ALU.mult, ALU.add))
            v.sem_inc(mean_ready, 1)
            v.wait_ge(rooted, 1)
            dve.link(v, newton(v, dve, rstd[:], sq[:], root[:], tmp[:]))
            v.wait_ge(y_landed, 16 * YT + 16)
            for n in range(YT):
                v.scalar_tensor_tensor(out=y[:, n], in0=y[:, n], scalar=rstd[:, n:n + 1], in1=dn_raw[:, 0],
                                       op0=ALU.mult, op1=ALU.mult).then_inc(y_done, 1)

        @block.tensor
        def _(pe):
            pe.wait_ge(h_ready, len(tiles))
            pe.sem_inc(upped, 2 * nb)
            pe.sem_inc(downed, 1)

            def project_up(i, s, half, ps_t, done):
                n0 = (i * 2 + s) * nb
                for b in range(nb):
                    if half == 0:
                        pe.wait_ge(gate_ready, n0 + b + 1)
                    else:
                        pe.wait_ge(prod_ready, n0 + nb + b + 1)
                    cs = slice(at[b], at[b + 1])
                    out = ps_t[:, b, 0:widths[b]]
                    for k in range(KT):
                        hi, lo = (w[:, s, k, half * P:(half + 1) * P] for w in (up_hi, up_lo))
                        pe.matmul(out, hi, h_hi[:, k, cs], start=(k == 0), stop=False)
                        pe.matmul(out, hi, h_lo[:, k, cs], start=False, stop=False)
                        last = pe.matmul(out, lo, h_hi[:, k, cs], start=False, stop=(k == KT - 1))
                    last.then_inc(done, 1)

            def body(i):
                pe.wait_ge(added, i * YT + 2)
                for s in range(2):
                    pe.wait_ge(up_ready, i * 2 + s + 3)
                    project_up(i, s, 0, g_ps, gated)
                for s in range(2):
                    project_up(i, s, 1, u_ps, upped)
                pe.wait_ge(dn_ready, i * 2 + 4)
                pe.wait_ge(gate_ready, (i + 1) * 2 * nb + nb)
                for n in range(YT):
                    need = next(b for b in range(nb) if at[b + 1] >= min((n + 1) * P, NT)) + 1
                    pe.wait_ge(prod_ready, (i * 2 + 1) * nb + 2 * nb + need)
                    pe.wait_ge(added, i * YT + n + 1)
                    for b in range(2):
                        cs = slice(b * 512, (b + 1) * 512)
                        ts = slice(n * P, (n + 1) * P)
                        for k in range(2):
                            pe.matmul(sums(n)[:, b], a_hi[:, k, ts], dn_hi[:, k, cs], start=(k == 0), stop=False)
                            pe.matmul(sums(n)[:, b], a_hi[:, k, ts], dn_lo[:, k, cs], start=False, stop=False)
                            last = pe.matmul(sums(n)[:, b], a_lo[:, k, ts], dn_hi[:, k, cs], start=False,
                                             stop=(k == 1))
                    last.then_inc(downed, 1)
            over_trips(pe, body)


RMAX = bass.bass_isa.ReduceOp.max


def bcast(ap_tensor, offset, dims, parts=P):
    return bass.AP(tensor=ap_tensor, offset=offset, ap=[[0, parts]] + dims)


def dilated_decode(nc, pa, consts_d, rel_d, onehot_d, caches, ma):
    NB2 = DEC * 2
    with ExitStack() as ctx:
        def sb(name, shape, dt=F32):
            return ctx.enter_context(nc.sbuf_tensor(f"dd_{name}", shape, dt))

        def ps(name, shape):
            return ctx.enter_context(nc.psum_tensor(f"dd_{name}_ps", shape, F32))

        def sem(name):
            return ctx.enter_context(nc.semaphore(f"dd_{name}"))

        ones = sb("ones", [P, P])
        rel = sb("rel", [BUCKETS, 2 * GROUPS])
        onehot = sb("onehot", [BUCKETS, GROUPS + 1, P])
        own = sb("own", [P, DEC, 3, A_WIDTH])
        kv = sb("kv", [P, GROUPS, DEC, 2, P])
        prod = sb("prod", [P, 2, DEC, P])
        bias = sb("bias", [P, 4, 2 * GROUPS])
        s = sb("s", [P, GROUPS, DEC, 2])
        s_own = sb("s_own", [P, GROUPS, DEC, 2])
        m = sb("m", [P, GROUPS, DEC, 2])
        p = sb("p", [P, GROUPS, DEC, 2])
        p_own = sb("p_own", [P, GROUPS, DEC, 2])
        row = sb("row", [1, GROUPS, DEC, P])
        stat = sb("stat", [1, GROUPS, DEC, 4])
        den_ps = ps("den", [P, 512])
        o_ps = ps("o", [P, 2, 2, 512])
        landed = sem("landed")
        bias_mm, s_ready, m_ready, p_ready, own_ready, exp_done = (sem(n) for n in (
            "bias_mm", "s_ready", "m_ready", "p_ready", "own_ready", "exp_done"))
        den_mm, weighed, o_mm, done, stored = (sem(n) for n in ("den_mm", "weighed", "o_mm", "done", "stored"))
        dve = Steps(sem("dve"))
        block = ctx.enter_context(nc.Block())

        @block.sync
        def _(sp):
            sp.dma_start(ones[:], consts_d[:, ONES]).then_inc(landed, 16)
            sp.dma_start(rel[:], rel_d[0:BUCKETS]).then_inc(landed, 16)
            sp.dma_start(onehot[:], onehot_d).then_inc(landed, 16)
            sp.dma_start(own[:].rearrange("p b k c -> p b (k c)"),
                         bcast(pa.tensor, 0, [[COLS_A, DEC], [1, 3 * A_WIDTH]])).then_inc(landed, 16)
            for g, (w, d) in enumerate(zip(WINDOWS, DILATIONS)):
                sp.dma_start(kv[:, g].rearrange("p b k c -> p b (k c)"),
                             caches[g].rearrange("b (i d) c -> i b d c", d=d)[:, :, 0]).then_inc(landed, 16)
            sp.wait_ge(done, 1)
            for g in range(GROUPS):
                sp.dma_start(ma[0:DEC, g * P:(g + 1) * P].rearrange("(a b) c -> a b c", a=1), row[:, g]
                             ).then_inc(stored, 16)
                sp.dma_start(ma[0:DEC, A_WIDTH + 4 * g:A_WIDTH + 4 * g + 4].rearrange("(a b) c -> a b c", a=1),
                             stat[:, g]).then_inc(stored, 16)
            sp.wait_ge(stored, 32 * GROUPS)

        @block.gpsimd
        def _(pool):
            pool.wait_ge(s_ready, 1)
            pool.partition_all_reduce(m[:].rearrange("p g b h -> p (g b h)"), s[:].rearrange("p g b h -> p (g b h)"),
                                      P, RMAX).then_inc(m_ready, 1)

        @block.scalar
        def _(act):
            act.wait_ge(p_ready, 1)
            act.activation(p[:], p[:], ACT.Exp)
            act.activation(p_own[:], p_own[:], ACT.Exp).then_inc(exp_done, 1)

        @block.vector
        def _(v):
            v.wait_ge(landed, 16 * 7)
            v.wait_ge(bias_mm, 1)
            dve.link(v, v.tensor_copy(bias[:].rearrange("p k h -> p (k h)"), den_ps[:, 0:4 * 2 * GROUPS]))
            for g in range(GROUPS):
                q = own[:, :, 0, g * P:(g + 1) * P]
                dve.link(v, v.tensor_tensor(prod[:, 0], kv[:, g, :, 0], q, ALU.mult))
                v.tensor_tensor(prod[:, 1], own[:, :, 1, g * P:(g + 1) * P], q, ALU.mult)
                dve.link(v, v.reduce_sum(s[:, g], prod[:, 0].rearrange("p b (h e) -> p b h e", e=HD), AX.X))
                dve.link(v, v.reduce_sum(s_own[:, g], prod[:, 1].rearrange("p b (h e) -> p b h e", e=HD), AX.X))
                for part, k in ((s, g), (s_own, GROUPS)):
                    last = v.scalar_tensor_tensor(out=part[:, g], in0=part[:, g], scalar=SCALE,
                                                  in1=bias[:, k, 2 * g:2 * g + 2].unsqueeze(1).to_broadcast([P, DEC, 2]),
                                                  op0=ALU.mult, op1=ALU.add)
                dve.link(v, last)
            v.sem_inc(s_ready, 1)
            v.wait_ge(m_ready, 1)
            dve.link(v, v.tensor_tensor(m[:], m[:], s_own[:], ALU.max))
            v.tensor_tensor(p_own[:], s_own[:], m[:], ALU.subtract)
            v.tensor_tensor(p[:], s[:], m[:], ALU.subtract).then_inc(p_ready, 1)
            v.wait_ge(exp_done, 1)
            for g in range(GROUPS):
                if g >= 2:
                    v.wait_ge(o_mm, g - 1)
                v.tensor_tensor(prod[:, g % 2].rearrange("p b (h e) -> p b h e", e=HD),
                                kv[:, g, :, 1].rearrange("p b (h e) -> p b h e", e=HD),
                                p[:, g].unsqueeze(3).to_broadcast([P, DEC, 2, HD]), ALU.mult).then_inc(weighed, 1)
            v.wait_ge(den_mm, 1)
            n = GROUPS * NB2
            v.tensor_tensor(stat[:, :, :, 2:4], den_ps[0:1, 0:n].rearrange("p (g b h) -> p g b h", g=GROUPS, h=2),
                            p_own[0:1], ALU.add)
            dve.link(v, v.tensor_copy(stat[:, :, :, 0:2], m[0:1]))
            for g in range(GROUPS):
                r = row[:, g].rearrange("p b (h e) -> p b h e", e=HD)
                dve.link(v, v.tensor_tensor(r, own[0:1, :, 2, g * P:(g + 1) * P].rearrange("p b (h e) -> p b h e", e=HD),
                                            p_own[0:1, g].unsqueeze(3).to_broadcast([1, DEC, 2, HD]), ALU.mult))
                v.wait_ge(o_mm, g + 1)
                flat = row[:, g].rearrange("p b c -> p (b c)").rearrange("p (a n) -> p a n", a=2)
                dve.link(v, v.tensor_tensor(flat, flat, o_ps[0:1, g % 2], ALU.add))
                v.sem_inc(own_ready, 1)
            v.sem_inc(done, 1)

        @block.tensor
        def _(pe):
            pe.wait_ge(landed, 16 * 7)
            for k in range(GROUPS + 1):
                last = pe.matmul(den_ps[:, k * 2 * GROUPS:(k + 1) * 2 * GROUPS], onehot[:, k], rel[:], start=True, stop=True)
            last.then_inc(bias_mm, 1)
            pe.wait_ge(exp_done, 1)
            n = GROUPS * NB2
            pe.matmul(den_ps[:, 0:n], ones[:], p[:].rearrange("p g b h -> p (g b h)"), start=True, stop=True
                      ).then_inc(den_mm, 1)
            for g in range(GROUPS):
                pe.wait_ge(weighed, g + 1)
                if g >= 2:
                    pe.wait_ge(own_ready, g - 1)
                for b in range(2):
                    last = pe.matmul(o_ps[:, g % 2, b], ones[:], prod[:, g % 2, 4 * b:4 * b + 4].rearrange(
                        "p b c -> p (b c)"), start=True, stop=True)
                last.then_inc(o_mm, 1)


def ssd_decode(nc, pb, consts_d, conv_rows_d, conv_state_d, heads_d, gates, state_d, bounce_d,
               s_ssm_d, s_conv_d, mc):
    H = C_HEADS
    XT = C_INNER // P
    NCV = C_CONV - 1
    with ExitStack() as ctx:
        def sb(name, shape, dt=F32):
            return ctx.enter_context(nc.sbuf_tensor(f"sd_{name}", shape, dt))

        def ps(name, shape):
            return ctx.enter_context(nc.psum_tensor(f"sd_{name}_ps", shape, F32))

        def sem(name):
            return ctx.enter_context(nc.semaphore(f"sd_{name}"))

        ident = sb("ident", [P, P])
        taps = sb("taps", [DEC, C_CONV + 1, CONV_DIM])
        heads = sb("heads", [DEC, 2, H])
        past = sb("past", [DEC, NCV, CONV_DIM])
        raw = sb("raw", [DEC, CDT])
        conv = sb("conv", [DEC, CONV_DIM])
        tmp = sb("tmp", [DEC, CONV_DIM])
        z = sb("z", [DEC, C_INNER])
        gates8 = sb("gates8", [DEC, 2, H])
        spread = sb("spread", [DEC, 3, H, HD])
        col = sb("col", [P, 3, XT, DEC])
        bc = sb("bc", [P, XT, 2, DEC, C_STATE])
        state = sb("state", [P, XT, DEC, C_STATE])
        upd = sb("upd", [P, XT, DEC, C_STATE])
        yT = sb("yT", [P, XT, DEC])
        y = sb("y", [DEC, MIX_C])
        junk = sb("junk", [DEC, C_INNER])
        t_ps = ps("t", [P, 512])
        y_ps = ps("y", [P, 512])
        landed, a_ready, exp_done, conv_ready, tanh_ready, bounced, bc_landed, spread_ready = (sem(n) for n in (
            "landed", "a_ready", "exp_done", "conv_ready", "tanh_ready", "bounced", "bc_landed", "spread_ready"))
        turned, state_ready, yT_ready, y_turned, y_ready, squared, stored, out_done = (sem(n) for n in (
            "turned", "state_ready", "yT_ready", "y_turned", "y_ready", "squared", "stored", "out_done"))
        dve = Steps(sem("dve"))
        block = ctx.enter_context(nc.Block())

        @block.sync
        def _(sp):
            sp.dma_start(ident[:], consts_d[:, IDENT]).then_inc(landed, 16)
            sp.dma_start(taps[:], bcast(conv_rows_d.tensor, 0, [[CONV_DIM, C_CONV + 1], [1, CONV_DIM]], DEC)
                         ).then_inc(landed, 16)
            sp.dma_start(heads[:], bcast(heads_d.tensor, 0, [[H, 2], [1, H]], DEC)).then_inc(landed, 16)
            sp.dma_start(past[:], conv_state_d).then_inc(landed, 16)
            sp.dma_start(raw[:], pb[0:DEC, 0:CDT]).then_inc(landed, 16)
            for t in range(XT):
                sp.dma_start(state[:, t], state_d[:, t * P:(t + 1) * P].rearrange("b p n -> p b n")
                             ).then_inc(landed, 16)
            sp.dma_start(s_conv_d[:, 0:NCV - 1], conv_state_d[:, 1:NCV]).then_inc(out_done, 16)
            sp.dma_start(s_conv_d[:, NCV - 1], pb[0:DEC, CX:CDT]).then_inc(out_done, 16)
            sp.wait_ge(conv_ready, 2)
            sp.dma_start(bounce_d, conv[:, C_INNER:]).then_inc(bounced, 16)
            sp.wait_ge(bounced, 16)
            W = 2 * C_GROUPS * C_STATE
            for t in range(XT):
                for half in range(2):
                    g = (2 * t + half) // (H // C_GROUPS)
                    for k in range(2):
                        sp.dma_start(bc[half * HD:(half + 1) * HD, t, k],
                                     bcast(bounce_d.tensor, (k * C_GROUPS + g) * C_STATE, [[W, DEC], [1, C_STATE]], HD)
                                     ).then_inc(bc_landed, 16)
            for t in range(XT):
                sp.wait_ge(state_ready, t + 1)
                sp.dma_start(s_ssm_d[:, t * P:(t + 1) * P].rearrange("b p n -> p b n"), state[:, t]
                             ).then_inc(out_done, 16)
            sp.wait_ge(squared, 1)
            sp.dma_start(mc[0:DEC, :], y[:]).then_inc(out_done, 16)
            sp.wait_ge(out_done, 16 * (XT + 3))

        @block.scalar
        def _(act):
            act.wait_ge(landed, 16 * (XT + 5))
            act.activation(heads[:, 0], heads[:, 0], ACT.Exp).then_inc(exp_done, 1)
            act.wait_ge(a_ready, 1)
            act.activation(gates8[:, 1], gates8[:, 1], ACT.Exp).then_inc(exp_done, 1)
            act.activation(z[:], raw[:, CZ:CX], ACT.Tanh, scale=0.5)
            act.wait_ge(conv_ready, 1)
            act.activation(tmp[:], conv[:], ACT.Tanh).then_inc(tanh_ready, 1)
            act.wait_ge(y_ready, 1)
            act.activation(junk[:], y[:, 0:C_INNER], ACT.Square, accum_out=y[:, C_INNER:MIX_C]).then_inc(squared, 1)

        @block.vector
        def _(v):
            v.wait_ge(landed, 16 * (XT + 5))
            dve.link(v, v.tensor_scalar(taps[:], taps[:], 0.5, None, ALU.mult))
            dve.link(v, v.tensor_tensor(conv[:], raw[:, CX:CDT], taps[:, NCV], ALU.mult))
            for j in range(NCV):
                dve.link(v, v.tensor_tensor(tmp[:], past[:, j], taps[:, j], ALU.mult))
                dve.link(v, v.tensor_tensor(conv[:], conv[:], tmp[:], ALU.add))
            v.tensor_tensor(conv[:], conv[:], taps[:, C_CONV], ALU.add).then_inc(conv_ready, 1)
            v.wait_ge(exp_done, 1)
            v.wait_ge(conv_ready, 1)
            dve.link(v, v.tensor_scalar(heads[:, 0], heads[:, 0], -1.0, None, ALU.mult))
            v.tensor_copy(gates8[:, 0], gates[0:DEC, 0, B_HEADS:B_HEADS + H])
            v.tensor_tensor(gates8[:, 1], gates[0:DEC, 0, B_HEADS:B_HEADS + H], heads[:, 0], ALU.mult
                            ).then_inc(a_ready, 1)
            v.wait_ge(tanh_ready, 1)
            v.wait_ge(exp_done, 2)
            v.wait_ge(a_ready, 1)
            v.scalar_tensor_tensor(out=conv[:], in0=tmp[:], scalar=1.0, in1=conv[:], op0=ALU.add, op1=ALU.mult
                                   ).then_inc(conv_ready, 1)
            v.wait_ge(conv_ready, 2)
            xs = conv[:, 0:C_INNER].rearrange("p (h e) -> p h e", e=HD)
            full = [DEC, H, HD]
            v.tensor_tensor(spread[:, 0], xs, gates8[:, 0].unsqueeze(2).to_broadcast(full), ALU.mult)
            v.tensor_copy(spread[:, 1], gates8[:, 1].unsqueeze(2).to_broadcast(full))
            v.tensor_tensor(spread[:, 2], xs, heads[:, 1].unsqueeze(2).to_broadcast(full), ALU.mult
                            ).then_inc(spread_ready, 1)
            dve.link(v, v.scalar_tensor_tensor(out=z[:], in0=z[:], scalar=1.0, in1=raw[:, CZ:CX],
                                               op0=ALU.add, op1=ALU.mult))
            v.wait_ge(turned, 1)
            dve.link(v, v.tensor_copy(col[:].rearrange("p k t b -> p (k t b)"), t_ps[:, 0:3 * XT * DEC]))
            v.wait_ge(bc_landed, 16 * 4 * XT)
            full = [P, DEC, C_STATE]
            for t in range(XT):
                v.tensor_tensor(upd[:, t], bc[:, t, 0], col[:, 0, t].unsqueeze(2).to_broadcast(full), ALU.mult)
                dve.link(v, v.tensor_tensor(state[:, t], state[:, t], col[:, 1, t].unsqueeze(2).to_broadcast(full),
                                            ALU.mult))
                v.tensor_tensor(state[:, t], state[:, t], upd[:, t], ALU.add).then_inc(state_ready, 1)
                v.wait_ge(state_ready, t + 1)
                dve.link(v, v.tensor_tensor(upd[:, t], state[:, t], bc[:, t, 1], ALU.mult))
                dve.link(v, v.reduce_sum(yT[:, t], upd[:, t], AX.X))
                dve.link(v, v.tensor_tensor(yT[:, t], yT[:, t], col[:, 2, t], ALU.add))
            v.sem_inc(yT_ready, 1)
            v.wait_ge(y_turned, 1)
            v.scalar_tensor_tensor(out=y[:, 0:C_INNER], in0=y_ps[0:DEC, 0:C_INNER], scalar=0.5, in1=z[:],
                                   op0=ALU.mult, op1=ALU.mult).then_inc(y_ready, 1)

        @block.tensor
        def _(pe):
            pe.wait_ge(landed, 16 * (XT + 5))
            pe.wait_ge(spread_ready, 1)
            for k in range(3):
                for t in range(XT):
                    c = (k * XT + t) * DEC
                    last = pe.transpose(t_ps[:, c:c + DEC], spread[:, k, 2 * t:2 * t + 2].rearrange("p h e -> p (h e)"),
                                        ident[0:DEC, 0:DEC])
            last.then_inc(turned, 1)
            pe.wait_ge(yT_ready, 1)
            for t in range(XT):
                last = pe.transpose(y_ps[0:DEC, t * P:(t + 1) * P], yT[:, t], ident[:])
            last.then_inc(y_turned, 1)


def fox_decode(nc, pa, consts_d, table_d, index_d, kv_d, logf_pool_d, logf_s_d, mb, lf_landed):
    F = B_WIDTH
    with ExitStack() as ctx:
        def sb(name, shape, dt=F32):
            return ctx.enter_context(nc.sbuf_tensor(f"fd_{name}", shape, dt))

        def ps(name, shape):
            return ctx.enter_context(nc.psum_tensor(f"fd_{name}_ps", shape, F32))

        def sem(name):
            return ctx.enter_context(nc.semaphore(f"fd_{name}"))

        consts = sb("consts", [P, 6, P])
        table = sb("table", [1, DEC * PAGES], I32)
        index = sb("index", [P, 2], I32)
        lf_row = sb("lf_row", [P, 2, PAGE * B_HEADS])
        lfT = sb("lfT", [P, 2, B_HEADS * P])
        page_sum = sb("page_sum", [P, 2, B_HEADS])
        page_sum_b = sb("page_sum_b", [P, 2, B_HEADS, P])
        idle = sb("idle", [1, 2])
        rest = sb("rest", [P, DEC, B_HEADS, PAGES])
        own = sb("own", [P, DEC, 3, F])
        logf = sb("logf", [P, DEC, B_HEADS])
        kv = sb("kv", [P, 2, PAGES, 2, F])
        prod = sb("prod", [P, 8, F])
        s = sb("s", [P, 2, B_HEADS, PAGES])
        s_own = sb("s_own", [P, DEC, B_HEADS])
        top = sb("top", [P, 2, B_HEADS])
        m = sb("m", [P, 2, B_HEADS])
        p = sb("p", [P, 2, B_HEADS, PAGES])
        p_own = sb("p_own", [P, 2, B_HEADS])
        v_own = sb("v_own", [1, 2, F])
        den = sb("den", [P, DEC, B_HEADS])
        oT = sb("oT", [P, 2, DEC])
        rden = sb("rden", [DEC, B_HEADS])
        out = sb("out", [DEC, F])
        big_ps = ps("big", [P, 2, 512])
        o_ps = ps("o", [P, 2, 2, 2])
        fin_ps = ps("fin", [P, 512])
        landed, lf_turned, lfT_ready, sums_ready, rest_mm, rest_ready = (sem(n) for n in (
            "landed", "lf_turned", "lfT_ready", "sums_ready", "rest_mm", "rest_ready"))
        kv_landed = [[sem(f"kv_landed{k}{e}") for e in range(2)] for k in range(2)]
        idle_set = sem("idle_set")
        top_ready, m_ready, p_in, p_ready, o_done, o_read, all_done, turned, den_mm, out_ready, stored = (
            sem(n) for n in ("top_ready", "m_ready", "p_in", "p_ready", "o_done", "o_read", "all_done", "turned",
                             "den_mm", "out_ready", "stored"))
        dve = Steps(sem("dve"))
        block = ctx.enter_context(nc.Block())

        def over_tokens(eng, body, steps=None, per=0):
            with eng.Fori(0, DEC // 2) as i:
                if steps:
                    with steps.loop(i, DEC // 2, per):
                        body(i, 0), body(i, 1)
                else:
                    body(i, 0), body(i, 1)

        def load_pages(eng, i, s_, e):
            for g in range(e, PAGES, 2):
                page = eng.value_load(table[0:1, bass.ds((i * 2 + s_) * PAGES + g, 1)], min_val=0,
                                      max_val=kv_d.shape[0] - 1)
                eng.dma_start(kv[:, s_, g].rearrange("p k c -> p (k c)"),
                              kv_d[bass.ds(page, 1)].rearrange("a p c -> (a p) c")).then_inc(kv_landed[s_][e], 16)

        @block.sync
        def _(sp):
            sp.dma_start(table[:], table_d).then_inc(landed, 16)
            sp.dma_start(consts[:], consts_d).then_inc(landed, 16)
            sp.dma_start(own[:].rearrange("p b k c -> p b (k c)"), bcast(pa.tensor, BQ, [[COLS_A, DEC], [1, 3 * F]])
                         ).then_inc(landed, 16)
            sp.dma_start(logf[:].rearrange("p b h -> p (b h)"), bcast(logf_s_d.tensor, 0, [[1, DEC * B_HEADS]])
                         ).then_inc(landed, 16)
            sp.wait_ge(landed, 64)

            def body(i, s_):
                sp.wait_ge(o_done, i * 2 + s_ + 1)
                load_pages(sp, i, s_, 0)
            over_tokens(sp, body)
            sp.wait_ge(out_ready, 1)
            sp.dma_start(mb[0:DEC, :], out[:]).then_inc(stored, 16)
            sp.wait_ge(stored, 16)

        @block.gpsimd
        def _(pool):
            pool.memset(idle[:], 0.0).then_inc(idle_set, 1)
            pool.wait_ge(idle_set, 1)
            pool.dma_start(index[:], index_d).then_inc(lf_landed, 16)
            pool.wait_ge(lf_landed, 16)
            for k in range(2):
                pool.indirect_dma_start(lf_row[:, k], None, logf_pool_d,
                                        bass.IndirectOffsetOnAxis(ap=index[:, k:k + 1], axis=0)).then_inc(lf_landed, 16)

            def body(i, s_):
                pool.wait_ge(top_ready, i * 2 + s_ + 1)
                pool.tensor_tensor(idle[:, 1:2], idle[:, 0:1], idle[:, 0:1], ALU.add)
                pool.partition_all_reduce(m[:, s_], top[:, s_], P, RMAX).then_inc(m_ready, 1)
            over_tokens(pool, body)

        @block.scalar
        def _(act):
            act.wait_ge(landed, 64)
            for s_ in range(2):
                load_pages(act, 0, s_, 1)

            def token(b, s_):
                act.wait_ge(p_in, b + 1)
                act.activation(p[:, s_], p[:, s_], ACT.Exp)
                act.activation(p_own[:, s_], p_own[:, s_], ACT.Exp).then_inc(p_ready, 1)

            with act.Fori(0, DEC // 2 - 1) as i:
                for s_ in range(2):
                    token(i * 2 + s_, s_)
                    act.wait_ge(o_done, i * 2 + s_ + 3)
                    load_pages(act, i + 1, s_, 1)
            for s_ in range(2):
                token(DEC - 2 + s_, s_)

        @block.vector
        def _(v):
            v.wait_ge(landed, 64)
            v.wait_ge(lf_landed, 48)
            for k in range(2):
                v.wait_ge(lf_turned, k + 1)
                v.tensor_copy(lfT[:, k], big_ps[:, k]).then_inc(lfT_ready, 1)
            dve.link(v, v.reduce_sum(page_sum[:], lf_row[:].rearrange("p k (n h) -> p k h n", h=B_HEADS), AX.X))
            v.tensor_copy(page_sum_b[:], page_sum[:].unsqueeze(3).to_broadcast([P, 2, B_HEADS, P])
                          ).then_inc(sums_ready, 1)
            v.wait_ge(rest_mm, 1)
            for k in range(2):
                dve.link(v, v.tensor_copy(rest[:, 4 * k:4 * k + 4].rearrange("p b h g -> p h b g"),
                                          big_ps[:, k].rearrange("p (h b g) -> p h b g", h=B_HEADS, g=PAGES)))
            for b in range(DEC):
                dve.link(v, v.tensor_tensor(prod[:, 0], own[:, b, 0], own[:, b, 1], ALU.mult))
                dve.link(v, v.reduce_sum(s_own[:, b], prod[:, 0].rearrange("p (h e) -> p h e", e=HD), AX.X))
            dve.link(v, v.tensor_scalar(s_own[:], s_own[:], SCALE, None, ALU.mult))

            def body(i, s_):
                b = i * 2 + s_
                for c in range(4):
                    if c == 0:
                        for e in range(2):
                            v.wait_ge(kv_landed[s_][e], i * (8 * PAGES) + 8 * PAGES)
                    dve.link(v, v.tensor_tensor(prod[:], kv[:, s_, 8 * c:8 * c + 8, 0],
                                                own[:, bass.ds(b, 1), 0].to_broadcast([P, 8, F]), ALU.mult))
                    dve.link(v, v.reduce_sum(s[:, s_, :, 8 * c:8 * c + 8].rearrange("p h g -> p g h"),
                                             prod[:].rearrange("p g (h e) -> p g h e", e=HD), AX.X))
                dve.link(v, v.scalar_tensor_tensor(
                    out=s[:, s_], in0=s[:, s_], scalar=SCALE,
                    in1=rest[:, bass.ds(b, 1)].rearrange("p b h g -> p (b h) g"), op0=ALU.mult, op1=ALU.add))
                dve.link(v, v.tensor_tensor(s[:, s_], s[:, s_], logf[:, bass.ds(b, 1)].rearrange("p b h -> p (b h)")
                                            .unsqueeze(2).to_broadcast([P, B_HEADS, PAGES]), ALU.add))
                v.reduce_max(top[:, s_], s[:, s_], AX.X).then_inc(top_ready, 1)
                v.wait_ge(m_ready, b + 1)
                dve.link(v, v.tensor_tensor(m[:, s_], m[:, s_], s_own[:, bass.ds(b, 1)].rearrange("p b h -> p (b h)"),
                                            ALU.max))
                v.wait_ge(o_done, b + 1)
                v.tensor_copy(v_own[0:1, s_], own[0:1, bass.ds(b, 1), 2].rearrange("p b c -> p (b c)"))
                v.tensor_tensor(p_own[:, s_], s_own[:, bass.ds(b, 1)].rearrange("p b h -> p (b h)"), m[:, s_],
                                ALU.subtract)
                v.tensor_tensor(p[:, s_], s[:, s_], m[:, s_].unsqueeze(2).to_broadcast([P, B_HEADS, PAGES]),
                                ALU.subtract).then_inc(p_in, 1)
                v.wait_ge(p_ready, b + 1)
                dve.link(v, v.reduce_sum(den[:, bass.ds(b, 1)].rearrange("p b h -> p (b h)"), p[:, s_], AX.X))
                v.wait_ge(o_done, b + 3)
                for t in range(2):
                    for h in range(2):
                        rows_ = slice(h * HD, (h + 1) * HD)
                        last = v.tensor_copy(oT[rows_, t, bass.ds(b, 1)], o_ps[rows_, t, s_, h:h + 1])
                last.then_inc(o_read, 1)
                first = den[0:1, bass.ds(b, 1)].rearrange("p b h -> p (b h)")
                dve.link(v, v.tensor_tensor(first, first, p_own[0:1, s_], ALU.add))
            over_tokens(v, body, dve, 2 * (8 + 5))
            v.wait_ge(o_read, DEC + 1)
            v.sem_inc(all_done, 1)
            v.wait_ge(den_mm, 1)
            dve.link(v, v.reciprocal(rden[:], fin_ps[0:DEC, 0:B_HEADS]))
            v.tensor_tensor(out[:].rearrange("p (h e) -> p h e", e=HD),
                            fin_ps[0:DEC, P:P + F].rearrange("p (h e) -> p h e", e=HD),
                            rden[:].unsqueeze(2).to_broadcast([DEC, B_HEADS, HD]), ALU.mult).then_inc(out_ready, 1)

        @block.tensor
        def _(pe):
            pe.wait_ge(landed, 64)
            pe.wait_ge(lf_landed, 48)
            for k in range(2):
                for h in range(B_HEADS):
                    last = pe.transpose(big_ps[:, k, h * P:(h + 1) * P],
                                        lf_row[:, k].rearrange("p (n h) -> p h n", h=B_HEADS)[:, h], consts[:, IDENT])
                last.then_inc(lf_turned, 1)
            pe.wait_ge(lfT_ready, 2)
            pe.wait_ge(sums_ready, 1)
            for k in range(2):
                pe.matmul(big_ps[:, k], consts[:, TRI_GT], lfT[:, k], start=True, stop=False)
                for h in range(B_HEADS):
                    last = pe.matmul(big_ps[:, k, h * P:(h + 1) * P], page_sum_b[:, k, h], consts[:, PAGE_AFTER],
                                     start=False, stop=(h == B_HEADS - 1))
            last.then_inc(rest_mm, 1)
            pe.sem_inc(o_done, 2)
            pe.sem_inc(o_read, 1)

            def body(i, s_):
                b = i * 2 + s_
                pe.wait_ge(p_ready, b + 1)
                pe.wait_ge(o_read, b + 1)
                for t in range(2):
                    for g in range(PAGES):
                        pe.matmul(o_ps[:, t, s_], kv[:, s_, g, 1, t * P:(t + 1) * P], p[:, s_, 2 * t:2 * t + 2, g],
                                  start=(g == 0), stop=False)
                    last = pe.matmul(o_ps[:, t, s_], v_own[0:1, s_, t * P:(t + 1) * P], p_own[0:1, s_, 2 * t:2 * t + 2],
                                     start=False, stop=True)
                last.then_inc(o_done, 1)
            over_tokens(pe, body)
            pe.wait_ge(all_done, 1)
            for h in range(B_HEADS):
                pe.matmul(fin_ps[0:DEC, h:h + 1], den[:, :, h], consts[:, ONES, 0:1], start=True, stop=True)
            for t in range(2):
                last = pe.transpose(fin_ps[0:DEC, P + t * P:P + (t + 1) * P], oT[:, t], consts[:, IDENT])
            last.then_inc(den_mm, 1)


def copy_caches(nc, caches, windows_out, state_ffn_d, s_ffn_old_d, copied):
    with nc.Block() as block:
        @block.gpsimd
        def _(pool):
            for cache, out in zip(caches, windows_out):
                w = cache.shape[1]
                pool.dma_start(out[:, 0:w - 1], cache[:, 1:w]).then_inc(copied, 16)
            pool.dma_start(s_ffn_old_d, state_ffn_d[:, 1]).then_inc(copied, 16)
    return 16 * (GROUPS + 1)


def copy_rows(nc, pa, windows_s, windows_p, fox_s, fox_p, mixes, new_rows):
    count = 16 * (4 * GROUPS + 2)
    with ExitStack() as ctx:
        ones = ctx.enter_context(nc.sbuf_tensor("cr_ones", [P, MIX_A], F32))
        filled = ctx.enter_context(nc.semaphore("cr_filled"))
        ones_stored = ctx.enter_context(nc.semaphore("cr_ones_stored"))
        block = ctx.enter_context(nc.Block())

        @block.vector
        def _(v):
            v.memset(ones[:], 1.0).then_inc(filled, 1)

        @block.scalar
        def _(act):
            for g, w in enumerate(WINDOWS):
                for k, col in enumerate((AK, AV)):
                    cols = slice(col + g * P, col + (g + 1) * P)
                    act.dma_start(windows_s[g][:, w - 1, k * P:(k + 1) * P], pa[0:DEC, cols]).then_inc(new_rows, 16)
                    act.dma_start(windows_p[g][:, k * P:(k + 1) * P], pa[P + SEQ - w:P + SEQ, cols]
                                  ).then_inc(new_rows, 16)
            act.dma_start(fox_s, pa[0:DEC, BK:FL]).then_inc(new_rows, 16)
            act.dma_start(fox_p, pa[P:P + SEQ, BK:FL]).then_inc(new_rows, 16)

        @block.sync
        def _(sp):
            sp.wait_ge(filled, 1)
            for mix in mixes:
                sp.dma_start(mix[DEC:P], ones[DEC:P, 0:mix.shape[1]]).then_inc(ones_stored, 16)
            sp.wait_ge(ones_stored, 16 * len(mixes))
    return count


def finish(nc, edge, p_ffn_d, copied, copied_count, new_rows, new_rows_count):
    with ExitStack() as ctx:
        stored = ctx.enter_context(nc.semaphore("fi_stored"))
        block = ctx.enter_context(nc.Block())

        @block.sync
        def _(sp):
            sp.dma_start(p_ffn_d, edge[:]).then_inc(stored, 16)
            sp.wait_ge(stored, 16)
            sp.wait_ge(copied, copied_count)
            sp.wait_ge(new_rows, new_rows_count)


def clear_semaphores(nc, kept):
    block = nc.Block()
    with block:
        @block.sync
        def _(sp):
            sp.sem_clear(range(max(s.num for s in kept) + 1, 256))


def program(nc, i, o):
    def scratch(name, shape):
        return nc.dram_tensor(name, shape, F32, kind="Internal").ap()

    T = ALL_TILES * P
    pa, pb = scratch("proj_a", [T, COLS_A]), scratch("proj_b", [T, COLS_B])
    ma, mb, mc = scratch("mix_a", [T, MIX_A]), scratch("mix_b", [T, B_WIDTH]), scratch("mix_c", [T, MIX_C])
    x2, h2 = scratch("x2", [T, D_MODEL]), scratch("h2", [ALL_TILES, P, KT, P])
    toep, bounce = scratch("toeplitz", [2 * GROUPS, P, 3 * P]), scratch("bc_rows", [DEC, 2 * C_GROUPS * C_STATE])
    caches = [i[f"cache{g}"] for g in range(GROUPS)]
    wins_s, wins_p = ([o[f"{s}_win{g}"] for g in range(GROUPS)] for s in "sp")
    with ExitStack() as ctx:
        copied = ctx.enter_context(nc.semaphore("copied"))
        new_rows = ctx.enter_context(nc.semaphore("new_rows"))
        logf_landed = ctx.enter_context(nc.semaphore("logf_landed"))
        blocks_landed = [ctx.enter_context(nc.semaphore(f"blocks_landed{u}")) for u in range(4)]
        kept = (copied, new_rows, logf_landed, *blocks_landed)
        gates = ctx.enter_context(nc.sbuf_tensor("gates", [P, ALL_TILES, B_HEADS + C_HEADS], F32))
        edge = ctx.enter_context(nc.sbuf_tensor("edge", [P, FF_TILES, FFN_CONV - 1], F32))
        rstd_all = ctx.enter_context(nc.sbuf_tensor("rstd_all", [P, ALL_TILES], F32))
        n_copied = copy_caches(nc, caches, wins_s, i["state_ffn"], o["s_ffn_old"], copied)
        project(nc, "pja", i["w_a"], i["xT"], i["x"], i["ln_mix"], pa, [480, 480, 480, 484], rstd_all, True)
        n_new = copy_rows(nc, pa, wins_s, wins_p, o["s_fox"], o["p_fox"], (ma, mb, mc), new_rows)
        project(nc, "pjb", i["w_b"], i["xT"], i["x"], i["ln_mix"], pb, [428, 428, 430], rstd_all, False)
        gate_values(nc, pa, pb, i["gate_bias"], gates, o["p_logf"], o["s_logf"])
        fox_prompt(nc, pa, i["consts"], gates, mb)
        clear_semaphores(nc, kept)
        dilated_prompt(nc, pa, i["consts"], i["rel"], i["dist_prompt"], toep, ma, blocks_landed)
        ssd_prompt(nc, pb, i["consts"], i["conv_cols"], i["heads"], gates, mc, o["p_ssm"], o["p_conv"])
        dilated_decode(nc, pa, i["consts"], i["rel"], i["dist_sample"], caches, ma)
        ssd_decode(nc, pb, i["consts"], i["conv_rows"], i["state_conv"], i["heads"], gates, i["state"], bounce,
                   o["s_ssm"], o["s_conv"], mc)
        fox_decode(nc, pa, i["consts"], i["table"], i["index"], i["fox_kv"], i["fox_logf"], o["s_logf"], mb,
                   logf_landed)
        clear_semaphores(nc, kept)
        out_project(nc, ma, mb, mc, i["x"], i["w_out"], i["consts"], i["norm_w"], i["ln_ffn"], x2, h2)
        for half in range(2):
            channel_mixer(nc, f"cm{half}", half == 0, 1 + half * (TILES // 2), h2, x2, i["w_up"], i["w_down"],
                          i["ffn_small"], i["final_w"], edge, o["y_p"], o["y_s"], o["s_gate"])
        finish(nc, edge, o["p_edge"], copied, n_copied, new_rows, n_new)


def bucket(dist):
    dist = np.asarray(dist)
    far = 16 + (np.log(np.maximum(dist, 1).astype(np.float32) / 16) / np.log(128.0).astype(np.float32) * 16
                ).astype(np.int32)
    return np.where(dist < 16, dist, np.minimum(far, BUCKETS - 1))


def constant_arrays():
    r = np.arange(P)
    k, n = r[:, None], r[None]
    squares = np.stack([k == n, k <= n, k > n, np.where(n > k, NEG, 0), np.ones((P, P)),
                        (k // PAGES == n // PAGES) & (k > n)]).astype(np.float32)
    prompt = np.zeros((BUCKETS + 1, GROUPS, 3 * P), np.float32)
    sample = np.zeros((BUCKETS, GROUPS + 1, P), np.float32)
    for g, d in enumerate(DILATIONS):
        for x in range(3 * P):
            steps = 2 * P - 1 - x
            if 0 <= steps <= P:
                prompt[bucket(steps * d), g, x] = 1
            else:
                prompt[BUCKETS, g, x] = NEG
        for x in range(P):
            sample[bucket((P - x) * d), g, x] = 1
    sample[0, GROUPS] = 1
    return np.ascontiguousarray(squares.transpose(1, 0, 2)), prompt, sample


def kernel(**inputs):
    import concourse.bacc as _bacc
    from concourse.bass_utils import run_bass_kernel_spmd as _run

    a = {k: np.asarray(v) for k, v in inputs.items()}
    x = np.zeros((ALL_TILES * P, D_MODEL), np.float32)
    x[:DEC] = a["x_sample"][:, 0]
    x[P:] = a["x_prompt"][0]
    w_in = a["w_in"][0].reshape(KT, P, -1).transpose(1, 0, 2)
    squares, prompt, sample = constant_arrays()
    split = lambda w, n: w.reshape(n, P).T
    conv_rows = np.concatenate([a["ssm_conv_w"][0], a["ssm_conv_b"]], 0)
    small = np.concatenate([a["ffn_conv_w"][0].reshape(FFN_CONV, FF_TILES, P).transpose(1, 2, 0),
                            a["ffn_conv_b"][0].reshape(FF_TILES, P, 1),
                            a["state_ffn_conv"][0].reshape(DEC, FFN_CONV - 1, FF_TILES, P).transpose(2, 3, 1, 0)
                            .reshape(FF_TILES, P, -1)], 2)
    arrays = {
        "x": x, "xT": x.reshape(ALL_TILES, P, KT, P).transpose(0, 3, 2, 1),
        "w_a": w_in[:, :, :COLS_A], "w_b": w_in[:, :, COLS_A:],
        "ln_mix": split(a["ln_mix_w"], KT), "ln_ffn": split(a["ln_ffn_w"], KT),
        "gate_bias": np.concatenate([a["fox_fgate_b"][0], a["ssm_dt_bias"][0]]),
        "consts": squares, "dist_prompt": prompt, "dist_sample": sample,
        "rel": np.concatenate([a["rel_bias"], np.ones((1, 2 * GROUPS), np.float32)]),
        "conv_rows": conv_rows,
        "conv_cols": conv_rows.reshape(C_CONV + 1, CONV_DIM // P, P).transpose(2, 1, 0),
        "heads": np.stack([a["ssm_A_log"][0], a["ssm_D"][0]]),
        "state": a["state_ssm"][0].reshape(DEC, C_INNER, C_STATE),
        "state_conv": a["state_ssm_conv"][0], "state_ffn": a["state_ffn_conv"][0],
        "table": a["page_table"].reshape(1, -1), "index": a["page_table"].reshape(2, P).T,
        "fox_kv": a["cache_fox_kv"][0].reshape(-1, PAGE, 2 * B_WIDTH),
        "fox_logf": a["cache_fox_logf"][0].reshape(-1, PAGE * B_HEADS),
        "w_out": a["w_out"][0].reshape(KT, P, D_MODEL).transpose(1, 0, 2),
        "norm_w": a["ssm_norm_w"][0],
        "w_up": a["w_up"][0].reshape(KT, P, 2, FF_TILES, P).transpose(3, 1, 0, 2, 4).reshape(FF_TILES, P, KT, 2 * P),
        "w_down": a["w_down"][0], "ffn_small": small, "final_w": a["final_norm_w"],
    }
    for g in range(GROUPS):
        arrays[f"cache{g}"] = a[f"cache_win{g}"][0].reshape(DEC, WINDOWS[g], 2 * P)
    outs = {
        "y_p": (SEQ, D_MODEL), "y_s": (DEC, D_MODEL), "p_fox": (SEQ, 2 * B_WIDTH), "s_fox": (DEC, 2 * B_WIDTH),
        "p_logf": (P, TILES, B_HEADS), "s_logf": (DEC, B_HEADS), "p_ssm": (C_INNER, C_STATE),
        "s_ssm": (DEC, C_INNER, C_STATE), "p_conv": (P, CONV_DIM // P, C_CONV - 1),
        "s_conv": (DEC, C_CONV - 1, CONV_DIM), "p_edge": (P, FF_TILES, FFN_CONV - 1),
        "s_ffn_old": (DEC, D_FF), "s_gate": (P, FF_TILES, DEC),
    }
    for g, w in enumerate(WINDOWS):
        outs[f"p_win{g}"] = (w, 2 * P)
        outs[f"s_win{g}"] = (DEC, w, 2 * P)
    arrays = {f"in_{k}": np.ascontiguousarray(v) for k, v in arrays.items()}
    nc = _bacc.Bacc("TRN2", target_bir_lowering=False, num_devices=1)
    ins = {k[3:]: nc.dram_tensor(k, v.shape, mybir.dt.from_np(v.dtype), kind="ExternalInput").ap()
           for k, v in arrays.items()}
    out_aps = {k: nc.dram_tensor(f"out_{k}", s, F32, kind="ExternalOutput").ap() for k, s in outs.items()}
    program(nc, ins, out_aps)
    r = _run(nc, [arrays], core_ids=[0]).results[0]
    r = {k: np.asarray(r[f"out_{k}"]) for k in outs}
    heads = lambda t, *lead: t.reshape(*lead, 2, -1, HD)
    win = lambda s, b: [heads(r[f"{s}_win{g}"], 1, b, w) for g, w in enumerate(WINDOWS)]
    return (r["y_p"].reshape(1, SEQ, D_MODEL), r["y_s"].reshape(DEC, 1, D_MODEL),
            *win("p", 1), heads(r["p_fox"], 1, 1, SEQ),
            r["p_logf"].transpose(1, 0, 2).reshape(1, 1, SEQ, B_HEADS),
            r["p_ssm"].reshape(1, 1, C_HEADS, HD, C_STATE),
            r["p_conv"].transpose(2, 1, 0).reshape(1, 1, C_CONV - 1, CONV_DIM),
            r["p_edge"].transpose(2, 1, 0).reshape(1, 1, FFN_CONV - 1, D_FF),
            *win("s", DEC), heads(r["s_fox"], 1, DEC, 1),
            r["s_logf"].reshape(1, DEC, 1, B_HEADS),
            r["s_ssm"].reshape(1, DEC, C_HEADS, HD, C_STATE), r["s_conv"].reshape(1, DEC, C_CONV - 1, CONV_DIM),
            np.stack([r["s_ffn_old"], r["s_gate"].transpose(2, 1, 0).reshape(DEC, D_FF)], 1)[None])
```
